# Optimizing a Trainium2 kernel written in Bass

```python
import jax, jax.numpy as jnp
from jax import lax
import numpy as np

D_MODEL = 1024
BATCH = 1
SEQ = 512
DEPTH = 2
DEC_BATCH = 8
DEC_SEQ = 16
PAST_LEN = 512

CHUNK = 64
N_META = 16
N_MIXERS = 2
N_GLA = (DEPTH + 1) // 2
N_CONV = DEPTH // 2
GLA_HEADS = 4
GLA_DK = D_MODEL // 2 // GLA_HEADS
GLA_DV = D_MODEL // GLA_HEADS
GLA_HK = GLA_HEADS * GLA_DK
GLA_HV = GLA_HEADS * GLA_DV
GLA_GATE_RANK = 16
GLA_TAU = 16.0
GLA_IN = 2 * GLA_HK + 2 * GLA_HV + GLA_GATE_RANK
CONV_W = 3
D_FF = 2816
EPS = 1e-6

kernel_name = "hybrid_gla_shortconv_convffn_stream_step"

def rmsnorm(x, g):
    xf = x.astype(jnp.float32)
    y = xf * lax.rsqrt(jnp.mean(xf * xf, axis=-1, keepdims=True) + EPS) * g.astype(jnp.float32)
    return y.astype(x.dtype)

def causal_dwconv(x, buf, w):
    L = x.shape[1]
    xp = jnp.concatenate([buf.astype(x.dtype), x], axis=1)
    y = xp[:, 0:L] * w[0]
    for j in range(1, CONV_W):
        y = y + xp[:, j:j + L] * w[j]
    return y, xp[:, -(CONV_W - 1):]

def gla_chunk(S, q, k, v, g):
    C = q.shape[1]
    b = jnp.cumsum(g, axis=1)
    o_inter = jnp.einsum('bthd,bhde->bthe', q * jnp.exp(b), S)
    mask = jnp.tril(jnp.ones((C, C), dtype=bool))
    rel = b[:, :, None] - b[:, None, :]
    decay = jnp.exp(jnp.where(mask[None, :, :, None, None], rel, -jnp.inf))
    A = jnp.einsum('bthd,bshd,btshd->bhts', q, k, decay)
    o_intra = jnp.einsum('bhts,bshe->bthe', A, v)
    b_last = b[:, -1]
    k_dec = k * jnp.exp(b_last[:, None] - b)
    S_new = jnp.exp(b_last)[..., None] * S + jnp.einsum('bshd,bshe->bhde', k_dec, v)
    return S_new, o_inter + o_intra

def gla_sequence(S0, q, k, v, g):
    B, L = q.shape[0], q.shape[1]
    lead = L % CHUNK
    S = S0
    outs = []
    if lead:
        S, o = gla_chunk(S, q[:, :lead], k[:, :lead], v[:, :lead], g[:, :lead])
        outs.append(o)
    n = (L - lead) // CHUNK
    if n:
        def to_blocks(a):
            a = a[:, lead:]
            return a.reshape((B, n, CHUNK) + a.shape[2:]).swapaxes(0, 1)

        def step(S_c, blk):
            return gla_chunk(S_c, *blk)

        S, o = lax.scan(step, S, (to_blocks(q), to_blocks(k), to_blocks(v), to_blocks(g)))
        o = o.swapaxes(0, 1).reshape((B, n * CHUNK) + o.shape[3:])
        outs.append(o)
    return S, jnp.concatenate(outs, axis=1)

def gla_mixer(h, S0, w_in, w_gate_up, b_gate, head_gain, w_out):
    B, L, _ = h.shape
    p = h @ w_in
    q, k, v, r, gdown = jnp.split(p, [GLA_HK, 2 * GLA_HK, 2 * GLA_HK + GLA_HV, 2 * GLA_HK + 2 * GLA_HV], axis=-1)
    q = q.reshape(B, L, GLA_HEADS, GLA_DK).astype(jnp.float32) * (GLA_DK ** -0.5)
    k = k.reshape(B, L, GLA_HEADS, GLA_DK).astype(jnp.float32)
    v = v.reshape(B, L, GLA_HEADS, GLA_DV).astype(jnp.float32)
    g = jax.nn.log_sigmoid((gdown @ w_gate_up + b_gate).astype(jnp.float32)) / GLA_TAU
    g = g.reshape(B, L, GLA_HEADS, GLA_DK)
    S, o = gla_sequence(S0.astype(jnp.float32), q, k, v, g)
    o = o * lax.rsqrt(jnp.mean(o * o, axis=-1, keepdims=True) + EPS) * head_gain.astype(jnp.float32)
    o = o.reshape(B, L, GLA_HV).astype(h.dtype) * jax.nn.silu(r)
    return o @ w_out, S.astype(h.dtype)

def shortconv_mixer(h, buf, w_in, conv_w, w_out):
    bg, cg, u = jnp.split(h @ w_in, 3, axis=-1)
    y, new_buf = causal_dwconv(cg * u, buf, conv_w)
    return (bg * y) @ w_out, new_buf

def conv_ffn(h, buf, w_up, conv_w, conv_b, w_down):
    z = h @ w_up
    zc, new_buf = causal_dwconv(z, buf, conv_w)
    gate, up = jnp.split(zc + conv_b, 2, axis=-1)
    return (jax.nn.silu(gate) * up) @ w_down, new_buf

def trunk(x, gla_S, conv_buf, ffn_buf, norm_mix, norm_ffn, norm_final,
          gla_w_in, gla_w_gate_up, gla_b_gate, gla_head_gain, gla_w_out,
          sc_w_in, sc_conv_w, sc_w_out, ffn_w_up, ffn_conv_w, ffn_conv_b, ffn_w_down):
    gla_new, conv_new, ffn_new = [], [], []
    for i in range(DEPTH):
        h = rmsnorm(x, norm_mix[i])
        j = i // N_MIXERS
        if i % N_MIXERS == 0:
            m, s = gla_mixer(h, gla_S[j], gla_w_in[j], gla_w_gate_up[j], gla_b_gate[j],
                             gla_head_gain[j], gla_w_out[j])
            gla_new.append(s)
        else:
            m, s = shortconv_mixer(h, conv_buf[j], sc_w_in[j], sc_conv_w[j], sc_w_out[j])
            conv_new.append(s)
        x = x + m
        f, s = conv_ffn(rmsnorm(x, norm_ffn[i]), ffn_buf[i], ffn_w_up[i], ffn_conv_w[i],
                        ffn_conv_b[i], ffn_w_down[i])
        ffn_new.append(s)
        x = x + f
    return rmsnorm(x, norm_final), jnp.stack(gla_new), jnp.stack(conv_new), jnp.stack(ffn_new)

def setup_inputs(seed: int = 0) -> dict:
    key = jax.random.key(seed)
    ks = jax.random.split(key, 24)

    def nrm(k, shape, scale):
        return jax.random.normal(k, shape, jnp.float32) * scale

    D, F2 = D_MODEL, 2 * D_FF
    return {
        "x_prompt": nrm(ks[0], (BATCH, SEQ, D), 1.0),
        "x_sample": nrm(ks[1], (DEC_BATCH, DEC_SEQ, D), 1.0),
        "state_gla": nrm(ks[2], (N_GLA, DEC_BATCH, GLA_HEADS, GLA_DK, GLA_DV), 1.0),
        "cache_conv": nrm(ks[3], (N_CONV, DEC_BATCH, CONV_W - 1, D), 1.0),
        "cache_ffn": nrm(ks[4], (DEPTH, DEC_BATCH, CONV_W - 1, F2), 1.0),
        "meta": nrm(ks[5], (N_META, D), 1.0),
        "norm_mix": 1.0 + nrm(ks[6], (DEPTH, D), 0.05),
        "norm_ffn": 1.0 + nrm(ks[7], (DEPTH, D), 0.05),
        "norm_final": 1.0 + nrm(ks[8], (D,), 0.05),
        "gla_w_in": nrm(ks[9], (N_GLA, D, GLA_IN), D ** -0.5),
        "gla_w_gate_up": nrm(ks[10], (N_GLA, GLA_GATE_RANK, GLA_HK), GLA_GATE_RANK ** -0.5),
        "gla_b_gate": nrm(ks[11], (N_GLA, GLA_HK), 0.1),
        "gla_head_gain": 1.0 + nrm(ks[12], (N_GLA, GLA_HEADS, GLA_DV), 0.05),
        "gla_w_out": nrm(ks[13], (N_GLA, GLA_HV, D), GLA_HV ** -0.5),
        "sc_w_in": nrm(ks[14], (N_CONV, D, 3 * D), D ** -0.5),
        "sc_conv_w": nrm(ks[15], (N_CONV, CONV_W, D), CONV_W ** -0.5),
        "sc_w_out": nrm(ks[16], (N_CONV, D, D), D ** -0.5),
        "ffn_w_up": nrm(ks[17], (DEPTH, D, F2), D ** -0.5),
        "ffn_conv_w": nrm(ks[18], (DEPTH, CONV_W, F2), CONV_W ** -0.5),
        "ffn_conv_b": nrm(ks[19], (DEPTH, F2), 0.01),
        "ffn_w_down": nrm(ks[20], (DEPTH, D_FF, D), D_FF ** -0.5),
    }

def reference(x_prompt, x_sample, state_gla, cache_conv, cache_ffn, meta, norm_mix, norm_ffn, norm_final,
              gla_w_in, gla_w_gate_up, gla_b_gate, gla_head_gain, gla_w_out,
              sc_w_in, sc_conv_w, sc_w_out, ffn_w_up, ffn_conv_w, ffn_conv_b, ffn_w_down):
    weights = (norm_mix, norm_ffn, norm_final, gla_w_in, gla_w_gate_up, gla_b_gate, gla_head_gain,
               gla_w_out, sc_w_in, sc_conv_w, sc_w_out, ffn_w_up, ffn_conv_w, ffn_conv_b, ffn_w_down)
    dt = x_prompt.dtype
    B = x_prompt.shape[0]
    xp = jnp.concatenate([jnp.broadcast_to(meta.astype(dt)[None], (B, N_META, D_MODEL)), x_prompt], axis=1)
    S0 = jnp.zeros((N_GLA, B, GLA_HEADS, GLA_DK, GLA_DV), dt)
    c0 = jnp.zeros((N_CONV, B, CONV_W - 1, D_MODEL), dt)
    f0 = jnp.zeros((DEPTH, B, CONV_W - 1, 2 * D_FF), dt)
    yp, gla_p, conv_p, ffn_p = trunk(xp, S0, c0, f0, *weights)
    y_prompt = yp[:, N_META:]
    y_sample, gla_s, conv_s, ffn_s = trunk(x_sample, state_gla, cache_conv, cache_ffn, *weights)
    return (y_prompt, y_sample, gla_p, gla_s, conv_p, conv_s, ffn_p, ffn_s)


_drawn_inputs = setup_inputs


def setup_inputs(seed=0):
    import zlib

    import numpy as np

    out = dict(_drawn_inputs(seed))
    spreads = {}
    factors = {'ffn_conv_b': 5.579}
    for name, (base, spread) in spreads.items():
        noise = np.random.default_rng([zlib.crc32(name.encode()), seed]).standard_normal(out[name].shape)
        drawn = base * np.exp(spread * noise) if base else spread * noise
        out[name] = __import__('jax').numpy.asarray(drawn.astype(out[name].dtype))
    for name, factor in factors.items():
        out[name] = (out[name] * factor).astype(out[name].dtype)
    return out
```

```python
import concourse.bass as bass
from concourse import mybir

F32 = mybir.dt.float32
F32R = mybir.dt.float32r
U8 = mybir.dt.uint8
I32 = mybir.dt.int32
ALU = mybir.AluOpType
ACT = mybir.ActivationFunctionType
AX = mybir.AxisListType

P = 128
D = 1024
KT = D // P
PROMPT = 16 + 512
SEQS, SLEN = 8, 16
SAMPLE = SEQS * SLEN
TOK = PROMPT + SAMPLE
HALF = TOK // 2
HP = PROMPT // 2
HEADS, DV = 4, 256
CH = 128
NCH = PROMPT // CH
TAIL = NCH * CH
FF = 2816
FT = FF // P
ZT = 2 * FT
PADDED = 2 + PROMPT + SEQS * (2 + SLEN)
SB = 2 + PROMPT
SW = 2 + SLEN
YN = PADDED - 2
LAST = PROMPT
ZW = LAST + (1 + SEQS) * SW
BANK = 512
RING = 4
TAU = 16.0
LEVELS = [1, 2, 4, 8, 16, 32, 64]
N_UNITS = 2 * HEADS + 16 + 8 + 2 * (ZT + FT) + 24 + 8
GROUPS = FT // 2
TRIPS = (GROUPS - 3) // 2
MIX_G = 4

C_NORM, C_BGATE, C_GAIN = 0, 40, 44
C_SCW, C_FFN = 52, 76
C_CCACHE = C_FFN + 2 * ZT * 4
C_EVEN = C_CCACHE + KT * 16
C_ODD, C_EPS = C_EVEN + 1, C_EVEN + 2
N_PAR = C_EVEN + 3


class SlotPlan:

    def __init__(self):
        self.used = [0] * RING
        self.next = 0
        self.steps = {}

    def straight(self, *names):
        for name in names:
            p = self.next % RING
            self.steps[name] = (p, self.used[p], 0)
            self.used[p] += 1
            self.next += 1

    def loop(self, names, trips):
        per = [0] * RING
        where = [(self.next + j) % RING for j in range(len(names))]
        for p in where:
            per[p] += 1
        seen = [0] * RING
        for name, p in zip(names, where):
            self.steps[name] = (p, self.used[p] + seen[p], per[p])
            seen[p] += 1
        for p in range(RING):
            self.used[p] += trips * per[p]
        self.next += len(names)

    def at(self, name, i=0):
        p, base, per = self.steps[name]
        return p, (base + per * i if per else base)


def plan_slots():
    s = SlotPlan()
    s.straight(("k", 0), ("q", 0), ("norm", 0), "gate_down")
    s.straight(*[("gate_up", h) for h in range(HEADS)])
    for h in range(1, HEADS):
        s.straight(("k", h), ("q", h))
    for h in range(HEADS):
        s.straight(("v", h, 0), ("A", h, 0), ("A", h, 1), ("v", h, 1), ("vT", h, 0), ("A", h, 2),
                   ("A", h, 3), ("r", h, 0), ("vT", h, 1), ("A", h, 4), ("A", h, 5), ("r", h, 1),
                   ("A", h, 6), ("A", h, 7))
    s.straight(("kT", 0))
    for h in range(HEADS):
        s.straight(*[("U", h, j) for j in range(4)])
        if h:
            s.straight(("head_norm", h - 1))
        if h + 1 < HEADS:
            s.straight(("kT", h + 1))
        s.straight(("o", h, 0), ("o", h, 1))
    s.straight(("head_norm", HEADS - 1))
    s.straight(*[("w_out", m) for m in range(KT)])
    for layer in range(2):
        if layer == 1:
            for g in range(MIX_G):
                for j in range(6):
                    s.straight(("mix", g, j))
                    if g == 0 and j == 1:
                        s.straight(("norm", 2))
                if g:
                    s.straight(*[("mix_out", g - 1, m) for m in range(KT)])
            s.straight(*[("mix_out", MIX_G - 1, m) for m in range(KT)])
        s.straight(("z", layer, 0, 0), ("z", layer, 0, 1), ("norm", 1 + 2 * layer),
                   ("z", layer, 0, 2), ("z", layer, 0, 3))
        s.straight(*[("z", layer, 1, j) for j in range(4)])
        body = []
        for g in range(2):
            body += [("down", layer, g, m) for m in range(KT)] + [("z", layer, 2 + g, j) for j in range(4)]
        s.loop(body, TRIPS)
        s.straight(*[("down", layer, 8, m) for m in range(KT)])
        s.straight(*[("z", layer, 10, j) for j in range(4)])
        s.straight(*[("down", layer, 9, m) for m in range(KT)])
        s.straight(*[("down", layer, 10, m) for m in range(KT)])
    s.straight(("norm", 4))
    return s


def build(nc, x_in, w_in, wgd_in, wgu_in, par_in, reset_in, mask_in, s0_in, zc_in,
          y_out, sp_out, ss_out, zl_out, cl_out):
    slots = plan_slots()

    base = (nc.sbuf_base + 31) // 32 * 32
    at = [base]

    def sb(name, shape, dt=F32, offset=None, size=None):
        if offset is not None:
            return nc.alloc_sbuf_tensor_at(name, shape, dt, offset=offset)
        n = 4
        for d in shape[1:]:
            n *= d
        t = nc.alloc_sbuf_tensor_at(name, shape, dt, offset=at[0])
        at[0] += (n + 31) // 32 * 32
        return t

    T4 = 4 * TOK
    x_at = at[0]
    x = sb("x", [P, KT, TOK])
    xh_at = at[0]
    xh = sb("xh", [P, KT, TOK], F32R)
    xl = sb("xl", [P, KT, TOK], F32R)
    raw = sb("raw", [P, RING, 8, P])
    wh = sb("wh", [P, RING, 8, P], F32R)
    wl = sb("wl", [P, RING, 8, P], F32R)
    par = sb("par", [P, N_PAR])
    rstd = sb("rstd", [P, TOK])
    ones = sb("ones", [P, P])
    ident = sb("ident", [P, P])
    turn = sb("turn", [P, 1])
    qk_at = at[0]
    qk = sb("qk", [P, 2 * HEADS, TOK])
    sr_at = at[0]
    sr = sb("sr", [P, KT, TOK])
    b_at = at[0]
    b = sb("b", [P, HEADS, TOK])
    vt_at = at[0]
    v_tok = sb("v_tok", [P, 6, D])
    AT_at = at[0]
    AT = sb("AT", [P, HEADS, TOK])
    spare = at[0]
    osq = sb("osq", [P, 2, TOK])
    dec = sb("dec", [P, HEADS, 13])
    gla_end = at[0]
    reset = sb("reset", [P, TOK], offset=AT_at)
    gd = sb("gd", [32, TOK], offset=AT_at + T4)
    wgu = sb("wgu", [32, 512], offset=AT_at + 2 * T4)
    wgd_raw = sb("wgd_raw", [P, KT, 16], offset=AT_at + 2 * T4 + 2048)
    wgd = sb("wgd", [P, KT, 32], F32R, offset=AT_at + 2 * T4 + 2560)
    pre = sb("pre", [P, HEADS, TOK], offset=sr_at)
    soft = sb("soft", [P, HEADS, TOK], offset=sr_at + 4 * T4)
    sq0 = sb("sq0", [P, KT, TOK], offset=b_at)
    lev = sb("lev", [P, 2, TOK], offset=x_at)
    dE = sb("dE", [P, 2, TOK], offset=x_at + 2 * T4)
    stage = sb("stage", [P, 2, TOK], offset=x_at + 4 * T4)
    mask_words = sb("mask", [P, 8 * TOK // 4], I32, offset=x_at + 6 * T4)
    mask = mask_words[:, :].bitcast(U8).rearrange("p (l t) -> p l t", l=8)
    s0 = sb("s0", [P, 2, SEQS, DV], offset=xh_at)
    snew = sb("snew", [P, 2, SEQS, DV], offset=xh_at + 16384)
    o32 = sb("o32", [P, 2, TOK], offset=xh_at + 32768)
    osum = sb("osum", [P, TOK], offset=xh_at + 32768 + 2 * T4)
    chain = sb("chain", [P, 5, DV], offset=b_at)
    kd = sb("kd", [P, 7, P], offset=b_at + 5120)
    oh = sb("oh", [P, KT, TOK], F32R, offset=sr_at)
    ol = sb("ol", [P, KT, TOK], F32R, offset=qk_at)
    at[0] = qk_at
    gh = sb("gh", [P, 4, TOK], F32R)
    gl = sb("gl", [P, 4, TOK], F32R)
    assert at[0] <= sr_at
    at[0] = sr_at
    y = sb("y", [P, 2, PADDED])
    sg = sb("sg", [P, PADDED])
    hh = sb("hh", [P, TOK])
    cg = sb("cg", [P, TOK])
    bg = sb("bg", [P, 2, TOK])
    assert at[0] <= b_at
    at[0] = b_at
    sq = sb("sq", [P, KT, TOK])
    zc = sb("zc", [P, 2 * ZT, 16])
    zl = sb("zl", [P, 2 * ZT, 18])
    cl = sb("cl", [P, KT, 18])
    zp = sb("zp", [P, 4, ZW])
    at[0] = max(at[0], gla_end)
    assert at[0] <= nc.sbuf_top

    ps = nc.alloc_psum_tensor("ps", [P, RING, 2 * BANK], F32)

    names = ["par_in", "gla_in", "wgd_done", "hi_done", "lo_done", "units_used", "consts",
             "xs_hi", "xs_lo", "sq_done", "sum_done", "std_done", "soft_done", "mask_in", "d_done", "e_done",
             "lev_done", "r_silu", "dec_done", "chain_stored", "osq_done", "osum_done", "o_done", "x_back",
             "zc_in", "pads_in", "y_done", "zl_saved", "gate_silu", "g_done", "cpads_in", "cy_done",
             "cl_saved", "out_done", "written", "tables_out"]
    sem = {n: nc.alloc_semaphore(n) for n in names}
    filled = [nc.alloc_semaphore(f"filled{i}") for i in range(RING)]
    freed = [nc.alloc_semaphore(f"freed{i}") for i in range(RING)]
    landed = [nc.alloc_semaphore(f"landed{i}") for i in range(RING)]
    x_in_s = [nc.alloc_semaphore(f"x_in{i}") for i in range(KT)]
    snew_stored = [nc.alloc_semaphore(f"snew_stored{i}") for i in range(2)]
    s0_in_s = [nc.alloc_semaphore(f"s0_in{i}") for i in range(2)]

    def two(ap):
        return ap.rearrange("p (h t) -> p h t", h=2)

    def slot(p, n=HALF):
        return ps[:, p, :].rearrange("p (h t) -> p h t", h=2)[:, :, 0:n]

    def blocks(ap, n):
        return ap.rearrange("p (n t) -> p n t", t=n)

    def norm_col(n, m):
        return par[:, C_NORM + 8 * n + m:C_NORM + 8 * n + m + 1]

    block = nc.Block()
    block.__enter__()

    @block.sync
    def _(sp):
        for k in range(KT):
            sp.dma_start(x[:, k, :], x_in[:, k, :]).then_inc(x_in_s[k], 16)
            if k == 0:
                sp.dma_start(par[:, :], par_in).then_inc(sem["par_in"], 16)
            if k < RING:
                sp.dma_start(raw[:, k, :, :], w_in[k]).then_inc(landed[k], 16)
        with sp.Fori(0, N_UNITS // RING - 1) as i:
            for j in range(RING):
                sp.wait_ge(sem["lo_done"], RING * i + j + 1)
                sp.dma_start(raw[:, j, :, :], w_in[bass.ds(RING * i + (RING + j), 1)]
                             .rearrange("u p m n -> p (u m) n")).then_inc(landed[j], 16)

    @block.gpsimd
    def _(pool):
        pool.memset(ones[:, :], 1.0)
        pool.memset(ident[:, :], 0.0)
        pool.drain()
        pool.affine_select(out=ident[:, :], in_=ident[:, :], compare_op=ALU.not_equal, fill=1.0, base=0,
                           pattern=[[-1, P]], channel_multiplier=1).then_inc(sem["consts"], 1)

        def split(j, n_landed, done):
            pool.wait_ge(landed[j], n_landed)
            pool.tensor_tensor(turn[:, :], ones[:, 0:1], ones[:, 0:1], ALU.mult)
            pool.tensor_copy(wh[:, j, :, :], raw[:, j, :, :]).then_inc(sem["hi_done"], 1)
            pool.wait_ge(sem["hi_done"], done)
            pool.tensor_tensor(wl[:, j, :, :], raw[:, j, :, :], wh[:, j, :, :].bitcast(F32),
                               ALU.subtract).then_inc(sem["lo_done"], 1)

        for j in range(RING):
            split(j, 16, j + 1)
        with pool.Fori(0, N_UNITS // RING - 1) as i:
            for j in range(RING):
                pool.wait_ge(sem["units_used"], RING * i + j + 1)
                split(j, 16 * i + 32, RING * i + (RING + j + 1))

    @block.tensor
    def _(pe):
        unit = [0]

        def open_slot(step, i=0):
            p, n = slots.at(step, i)
            if not (isinstance(n, int) and n == 0):
                pe.wait_ge(freed[p], n)
            return p

        def copied(step):
            p, n = slots.at(step)
            pe.wait_ge(freed[p], n + 1)

        def weights(n_ready):
            pe.wait_ge(sem["lo_done"], n_ready)

        def project(step, hi, lo, n_ready, ring, cut, i=0, release=1, before=None):
            p = open_slot(step, i)
            weights(n_ready)
            halves = ((0, 0, cut), (BANK, cut, TOK))
            for k in range(KT):
                if before:
                    before(k)
                for w, v in ((wh, hi), (wh, lo), (wl, hi)):
                    for c, a, z in halves:
                        first = k == 0 and w is wh and v is hi
                        mm = pe.matmul(ps[:, p, c:c + z - a], w[:, ring, k, :], v[:, k, a:z], start=first,
                                       stop=(k == KT - 1 and w is wl))
                        if k == 0 and w is wh and v is hi and c and release:
                            mm.then_inc(sem["units_used"], release)
            mm.then_inc(filled[p], 1)

        def project_down(step, f0, n_ready, rings, i=0, release=1, g_count=None):
            weights(n_ready)
            pe.wait_ge(sem["g_done"], g_count)
            for m in range(KT):
                p = open_slot(step(m), i)
                for f in range(2):
                    for w, v in ((wh, gh), (wh, gl), (wl, gh)):
                        for c, a in ((0, 0), (BANK, HALF)):
                            mm = pe.matmul(ps[:, p, c:c + HALF], w[:, rings[f], m, :], v[:, f0 + f, a:a + HALF],
                                           start=(f == 0 and w is wh and v is gh), stop=(f == 1 and w is wl))
                            if m == 0 and f == 0 and w is wh and v is gh and c:
                                mm.then_inc(sem["units_used"], release)
                mm.then_inc(filled[p], 1)

        def norm_sum(n):
            p = open_slot(("norm", n))
            pe.wait_ge(sem["sum_done"], n + 1)
            src = osq[:, 0, :] if n == 0 else hh
            for c, a in ((0, 0), (BANK, HALF)):
                mm = pe.matmul(ps[:, p, c:c + HALF], ones[:, :], src[:, a:a + HALF], start=True, stop=True)
            mm.then_inc(filled[p], 1)

        n_unit = 0

        def x_ready(n):
            return lambda k: pe.wait_ge(sem["xs_lo"], KT * n + k + 1)

        pe.wait_ge(sem["consts"], 1)
        for h in range(HEADS):
            for j, kind in enumerate("kq"):
                project((kind, h), xh, xl, n_unit + 1, n_unit % RING, HALF, release=1 if n_unit else 0,
                        before=x_ready(0) if n_unit == 0 else None)
                n_unit += 1
            if h == 0:
                norm_sum(0)
                p = open_slot("gate_down")
                pe.wait_ge(sem["wgd_done"], 1)
                for k in range(KT):
                    for v in (xh, xl):
                        for c, a in ((0, 0), (BANK, HALF)):
                            mm = pe.matmul(ps[0:32, p, c:c + HALF], wgd[:, k, :], v[:, k, a:a + HALF],
                                           start=(k == 0 and v is xh), stop=(k == KT - 1 and v is xl))
                mm.then_inc(filled[p], 1)
                copied("gate_down")
                pe.wait_ge(sem["gla_in"], 48)
                for g in range(HEADS):
                    p = open_slot(("gate_up", g))
                    for c, a in ((0, 0), (BANK, HALF)):
                        mm = pe.matmul(ps[:, p, c:c + HALF], wgu[:, g * P:(g + 1) * P], gd[:, a:a + HALF],
                                       start=True, stop=True)
                    mm.then_inc(filled[p], 1)

        def scores(h, lv):
            p = open_slot(("A", h, lv))
            if lv == 0:
                ks, qs = qk[:, 2 * h, :], qk[:, 2 * h + 1, :]
                copied(("k", h))
                copied(("q", h))
            else:
                ks = qs = lev[:, (lv - 1) % 2, :]
                pe.wait_ge(sem["lev_done"], 9 * h + lv)
            for c in range(NCH):
                mm = pe.matmul(ps[:, p, c * CH:(c + 1) * CH], ks[:, c * CH:(c + 1) * CH],
                               qs[:, c * CH:(c + 1) * CH], start=True, stop=True)
            if lv == 0 or LEVELS[lv - 1] < SLEN:
                pe.matmul(ps[:, p, TAIL:PROMPT], ks[:, TAIL:TAIL + P], qs[:, TAIL:PROMPT], start=True, stop=True)
                mm = pe.matmul(ps[:, p, PROMPT:TOK], ks[:, PROMPT:TOK], qs[:, PROMPT:TOK], start=True, stop=True)
            mm.then_inc(filled[p], 1)

        starts = [c * CH for c in range(NCH)] + [TAIL, PROMPT]

        def to_tokens(step, src):
            p = open_slot(step)
            for t, a in enumerate(starts):
                mm = pe.transpose(ps[:, p, t * P:(t + 1) * P], src[:, a:a + P], ident[:, :])
            mm.then_inc(filled[p], 1)

        def value(kind, h, e):
            nonlocal n_unit
            project((kind, h, e), xh, xl, n_unit + 1, n_unit % RING, HALF)
            n_unit += 1

        def transpose_v(h, e):
            copied(("v", h, e))
            to_tokens(("vT", h, e), stage[:, e, :])

        for h in range(HEADS):
            value("v", h, 0)
            scores(h, 0)
            scores(h, 1)
            value("v", h, 1)
            transpose_v(h, 0)
            scores(h, 2)
            scores(h, 3)
            value("r", h, 0)
            transpose_v(h, 1)
            scores(h, 4)
            scores(h, 5)
            value("r", h, 1)
            scores(h, 6)
            scores(h, 7)

        def transpose_k(h):
            pe.wait_ge(sem["lev_done"], 9 * h + 8)
            to_tokens(("kT", h), qk[:, 2 * h, :])

        def update(h, j, n, lhsT, rhs):
            p, _ = slots.at(("U", h, j))
            return pe.matmul(ps[:, p, n * DV:(n + 1) * DV], lhsT, rhs, start=True, stop=True,
                             skip_group_check=True), p

        transpose_k(0)
        for h in range(HEADS):
            vs = slice(h * DV, (h + 1) * DV)
            copied(("kT", h))
            for e in range(2):
                copied(("vT", h, e))
            open_slot(("U", h, 0))
            for c in range(NCH):
                mm, p = update(h, 0, c, kd[:, c, :], v_tok[:, c, vs])
            mm.then_inc(filled[p], 1)
            for j in (1, 2):
                open_slot(("U", h, j))
                for n in range(4):
                    s = 4 * (j - 1) + n
                    rows = slice(32 * (s // 2), 32 * (s // 2) + 32)
                    mm, p = update(h, j, n, kd[rows, 5 + s % 2, :], v_tok[rows, 5, vs])
                mm.then_inc(filled[p], 1)
            open_slot(("U", h, 3))
            mm, p = update(h, 3, 0, kd[0:16, 4, :], v_tok[0:16, 4, vs])
            mm.then_inc(filled[p], 1)
            if h:
                head_norm_step = ("head_norm", h - 1)
                p = open_slot(head_norm_step)
                pe.wait_ge(sem["osum_done"], h)
                for c, a in ((0, 0), (BANK, HALF)):
                    mm = pe.matmul(ps[:, p, c:c + HALF], ones[:, :], osum[:, a:a + HALF], start=True, stop=True)
                mm.then_inc(filled[p], 1)
            if h + 1 < HEADS:
                transpose_k(h + 1)
            copied(("U", h, 0))
            pe.wait_ge(s0_in_s[h % 2], 16 * (h // 2 + 1))
            pe.wait_ge(sem["lev_done"], 9 * h + 9)
            copied(("A", h, 7))
            q = qk[:, 2 * h + 1, :]
            for e in range(2):
                p = open_slot(("o", h, e))
                es = slice(h * DV + e * P, h * DV + (e + 1) * P)
                ee = slice(e * P, (e + 1) * P)

                def mm_o(a, z, lhsT, rhs, start, stop):
                    return pe.matmul(ps[:, p, a:z], lhsT, rhs, start=start, stop=stop, skip_group_check=True)

                for c in range(NCH):
                    a, z = c * CH, (c + 1) * CH
                    mm_o(a, z, v_tok[:, c, es], AT[:, h, a:z], True, c == 0)
                    if c:
                        mm_o(a, z, chain[:, c - 1, ee], q[:, a:z], False, True)
                mm_o(TAIL, PROMPT, v_tok[0:16, 4, es], AT[0:16, h, TAIL:PROMPT], True, False)
                mm_o(TAIL, PROMPT, chain[:, 3, ee], q[:, TAIL:PROMPT], False, True)
                mm_o(PROMPT, TOK, v_tok[:, 5, es], AT[:, h, PROMPT:TOK], True, False)
                for s in range(SEQS):
                    a = PROMPT + s * SLEN
                    mm = mm_o(a, a + SLEN, s0[:, h % 2, s, ee], q[:, a:a + SLEN], False, s == SEQS - 1)
                mm.then_inc(filled[p], 1)
        p = open_slot(("head_norm", HEADS - 1))
        pe.wait_ge(sem["osum_done"], HEADS)
        for c, a in ((0, 0), (BANK, HALF)):
            mm = pe.matmul(ps[:, p, c:c + HALF], ones[:, :], osum[:, a:a + HALF], start=True, stop=True)
        mm.then_inc(filled[p], 1)

        for m in range(KT):
            project(("w_out", m), oh, ol, n_unit + 1, n_unit % RING, HALF,
                    before=(lambda k: k % 2 or pe.wait_ge(sem["o_done"], k // 2 + 1)) if m == 0 else None)
            n_unit += 1

        g_before = 0
        for layer in range(2):
            if layer == 1:
                for g in range(MIX_G):
                    for j in range(6):
                        project(("mix", g, j), xh, xl, n_unit + 1, n_unit % RING, HALF,
                                release=2 if j == 0 and (g != 1) else 1,
                                before=x_ready(2) if g == 0 and j == 0 else None)
                        n_unit += 1
                        if g == 0 and j == 1:
                            norm_sum(2)
                    if g:
                        project_down(lambda m, g=g: ("mix_out", g - 1, m), 2 * ((g - 1) % 2), n_unit + 2,
                                     [n_unit % RING, (n_unit + 1) % RING], g_count=g_before + 2 * g)
                        n_unit += 2
                project_down(lambda m: ("mix_out", MIX_G - 1, m), 2 * ((MIX_G - 1) % 2), n_unit + 2,
                             [n_unit % RING, (n_unit + 1) % RING], release=2, g_count=g_before + 2 * MIX_G)
                n_unit += 2
                g_before += 2 * MIX_G
            def z_units(g, i=0, release=1, norm=None):
                nonlocal n_unit
                for j in range(4):
                    u = n_unit + j
                    project(("z", layer, g, j), xh, xl, 12 * i + (u + 1), u % RING, HP, i=i,
                            release=release if j == 0 else 1,
                            before=x_ready(norm) if norm is not None and j == 0 else None)
                    if norm is not None and j == 1:
                        norm_sum(norm)
                n_unit += 4

            def down_units(g, count, i=0, release=1):
                nonlocal n_unit
                u = n_unit
                project_down(lambda m: ("down", layer, g, m), 2 * (g % 2), 12 * i + (u + 2),
                             [u % RING, (u + 1) % RING], i=i, release=release, g_count=count)
                n_unit += 2

            z_units(0, release=2 if layer else 1, norm=1 + 2 * layer)
            z_units(1)
            with pe.Fori(0, TRIPS) as i:
                for g in range(2):
                    down_units(g, 4 * i + (g_before + 2 * g + 2), i=i)
                    z_units(2 + g, i=i, release=2)
            n_unit += 12 * (TRIPS - 1)
            down_units(8, g_before + 18)
            z_units(10, release=2)
            down_units(9, g_before + 20)
            down_units(10, g_before + 22, release=2)
            g_before += FT
        norm_sum(4)
        assert n_unit == N_UNITS

    @block.vector
    def _(dve):
        def take(step, i=0):
            p, n = slots.at(step, i)
            dve.wait_ge(filled[p], n + 1)
            return p

        def split_low(n, m):
            dve.wait_ge(sem["xs_hi"], KT * min(n, 3) + m + 1)
            dve.scalar_tensor_tensor(out=xl[:, m, :], in0=x[:, m, :], scalar=norm_col(n, m),
                                     in1=xh[:, m, :].bitcast(F32), op0=ALU.mult,
                                     op1=ALU.subtract).then_inc(sem["xs_lo"], 1)

        def sum_squares(n):
            dve.wait_ge(sem["sq_done"], KT * (n + 1))
            src, out = (sq0, osq[:, 0, :]) if n == 0 else (sq, hh[:, :])
            dve.tensor_reduce(out, src[:, :, :].rearrange("p k t -> p t k"), AX.X,
                              ALU.add).then_inc(sem["sum_done"], 1)

        def invert_std(n):
            dve.wait_ge(sem["std_done"], n + 1)
            dve.reciprocal(rstd[:, :], rstd[:, :])
            dve.drain()

        def update_x(steps, n):
            for m in range(KT):
                p = take(steps(m))
                dve.tensor_tensor(two(x[:, m, :]), slot(p), two(x[:, m, :]), ALU.add).then_inc(freed[p], 1)
                if m and n < 4:
                    split_low(n, m - 1)
            if n < 4:
                split_low(n, KT - 1)
            sum_squares(n)

        dve.wait_ge(sem["par_in"], 16)
        for m in range(KT):
            split_low(0, m)
        sum_squares(0)
        dve.wait_ge(sem["gla_in"], 48)
        dve.tensor_copy(wgd[:, :, 0:16], wgd_raw[:, :, :])
        dve.drain()
        dve.tensor_tensor(wgd[:, :, 16:32], wgd_raw[:, :, :], wgd[:, :, 0:16].bitcast(F32),
                          ALU.subtract).then_inc(sem["wgd_done"], 1)
        invert_std(0)

        def take_kq(h):
            p = take(("k", h))
            dve.tensor_tensor(two(qk[:, 2 * h, :]), slot(p), two(rstd[:, :]), ALU.mult).then_inc(freed[p], 1)
            p = take(("q", h))
            dve.scalar_tensor_tensor(out=two(qk[:, 2 * h + 1, :]), in0=slot(p), scalar=float(P) ** -0.5,
                                     in1=two(rstd[:, :]), op0=ALU.mult, op1=ALU.mult).then_inc(freed[p], 1)

        take_kq(0)
        p = take("gate_down")
        dve.tensor_tensor(two(gd[:, :]), slot(p)[0:32], two(rstd[0:32, :]), ALU.mult).then_inc(freed[p], 1)
        for h in range(HEADS):
            p = take(("gate_up", h))
            dve.tensor_scalar(two(pre[:, h, :]), slot(p), par[:, C_BGATE + h:C_BGATE + h + 1], None,
                              ALU.add).then_inc(freed[p], 1)
        take_kq(1)
        dve.wait_ge(sem["soft_done"], 1)
        dve.scalar_tensor_tensor(out=pre[:, :, :], in0=pre[:, :, :], scalar=0.0, in1=soft[:, :, :],
                                 op0=ALU.min, op1=ALU.subtract)
        dve.drain()
        for h in range(HEADS):
            dve.tensor_tensor_scan(b[:, h, :], reset[:, :], pre[:, h, :], 0.0, ALU.mult, ALU.add)
        dve.drain()
        take_kq(2)
        take_kq(3)

        def width(t):
            return TOK if LEVELS[t] < SLEN else TAIL

        def distance(h, t):
            if t < 7:
                m, w = LEVELS[t], width(t)
                bb = blocks(b[:, h, 0:w], 2 * m)
                ref = bb[:, :, m - 1:m].to_broadcast([P, w // (2 * m), 2 * m])
                dve.tensor_tensor(blocks(dE[:, t % 2, 0:w], 2 * m), bb, ref,
                                  ALU.subtract).then_inc(sem["d_done"], 1)
                return
            for a, z, m in ((0, TAIL, CH), (TAIL, TOK, SLEN)):
                bb = blocks(b[:, h, a:z], m)
                ref = bb[:, :, m - 1:m].to_broadcast([P, (z - a) // m, m])
                last = dve.tensor_tensor(blocks(dE[:, t % 2, a:z], m), ref, bb, ALU.subtract)
            last.then_inc(sem["d_done"], 1)

        def decayed(h, t):
            dve.wait_ge(sem["e_done"], 9 * h + t + 1)
            k, q = qk[:, 2 * h, :], qk[:, 2 * h + 1, :]
            if t < 7:
                m, w = LEVELS[t], width(t)
                for src, part in ((k, slice(0, m)), (q, slice(m, 2 * m))):
                    last = dve.tensor_tensor(blocks(lev[:, t % 2, 0:w], 2 * m)[:, :, part],
                                             blocks(dE[:, t % 2, 0:w], 2 * m)[:, :, part],
                                             blocks(src[:, 0:w], 2 * m)[:, :, part], ALU.mult)
            else:
                src = k if t == 7 else q
                last = dve.tensor_tensor(src, src, dE[:, t % 2, :], ALU.mult)
            last.then_inc(sem["lev_done"], 1)

        def keep(h, lv):
            p = take(("A", h, lv))
            w = TOK if lv == 0 else width(lv - 1)
            dve.copy_predicated(AT[:, h, 0:w], mask[:, lv, 0:w], ps[:, p, 0:w]).then_inc(freed[p], 1)

        def take_value(kind, h, e):
            if kind == "v" and h:
                dve.wait_ge(sem["r_silu"], 2 * (h - 1) + e + 1)
            if kind == "r":
                take(("vT", h, e))
            p = take((kind, h, e))
            dve.tensor_tensor(two(stage[:, e, :]), slot(p), two(rstd[:, :]), ALU.mult).then_inc(freed[p], 1)

        for h in range(HEADS):
            dve.memset(AT[:, h, :], 0.0)
            distance(h, 0)
            distance(h, 1)
            decayed(h, 0)
            if h == 0:
                dve.wait_ge(sem["mask_in"], 16)
            for n, (kind, e) in enumerate((("v", 0), ("v", 1), ("r", 0), ("r", 1))):
                take_value(kind, h, e)
                dve.drain()
                keep(h, 2 * n)
                if n < 3:
                    distance(h, 2 * n + 2)
                decayed(h, 2 * n + 1)
                dve.drain()
                keep(h, 2 * n + 1)
                if n < 3:
                    distance(h, 2 * n + 3)
                decayed(h, 2 * n + 2)
            dve.drain()

        def finish(h):
            p, n = slots.at(("head_norm", h))
            dve.wait_ge(freed[p], n + 1)
            dve.reciprocal(osq[:, 0, :], osq[:, 0, :])
            dve.drain()
            dve.tensor_tensor(o32[:, :, :], o32[:, :, :],
                              osq[:, 0:1, :].to_broadcast([P, 2, TOK]), ALU.mult)
            dve.drain()
            dve.tensor_copy(oh[:, 2 * h:2 * h + 2, :], o32[:, :, :])
            dve.drain()
            dve.tensor_tensor(ol[:, 2 * h:2 * h + 2, :], o32[:, :, :],
                              oh[:, 2 * h:2 * h + 2, :].bitcast(F32), ALU.subtract).then_inc(sem["o_done"], 1)

        for h in range(HEADS):
            dve.wait_ge(sem["dec_done"], h + 1)
            if h:
                dve.wait_ge(sem["chain_stored"], 16 * h)
            p = take(("U", h, 0))
            dve.tensor_copy(chain[:, 0, :], ps[:, p, 0:DV])
            dve.drain()
            for c in range(1, NCH):
                ins = dve.scalar_tensor_tensor(out=chain[:, c, :], in0=chain[:, c - 1, :],
                                               scalar=dec[:, h, c:c + 1], in1=ps[:, p, c * DV:(c + 1) * DV],
                                               op0=ALU.mult, op1=ALU.add)
                if c == NCH - 1:
                    ins.then_inc(freed[p], 1)
                dve.drain()
            dve.wait_ge(s0_in_s[h % 2], 16 * (h // 2 + 1))
            if h >= 2:
                dve.wait_ge(snew_stored[h % 2], 16)
            for s in range(SEQS):
                n = s % 4
                if n == 0:
                    p = take(("U", h, 1 + s // 4))
                ins = dve.scalar_tensor_tensor(out=snew[:, h % 2, s, :], in0=s0[:, h % 2, s, :],
                                               scalar=dec[:, h, 5 + s:6 + s], in1=ps[:, p, n * DV:(n + 1) * DV],
                                               op0=ALU.mult, op1=ALU.add)
                if n == 3:
                    ins.then_inc(freed[p], 1)
            p = take(("U", h, 3))
            dve.scalar_tensor_tensor(out=chain[:, 4, :], in0=chain[:, 3, :], scalar=dec[:, h, 4:5],
                                     in1=ps[:, p, 0:DV], op0=ALU.mult, op1=ALU.add).then_inc(freed[p], 1)
            if h:
                finish(h - 1)
            for e in range(2):
                p = take(("o", h, e))
                dve.wait_ge(sem["osq_done"], 2 * h + e + 1)
                if e == 0:
                    dve.drain()
                dve.scalar_tensor_tensor(out=o32[:, e, :], in0=ps[:, p, 0:TOK],
                                         scalar=par[:, C_GAIN + 2 * h + e:C_GAIN + 2 * h + e + 1],
                                         in1=sr[:, 2 * h + e, :], op0=ALU.mult,
                                         op1=ALU.mult).then_inc(freed[p], 1)
            dve.tensor_tensor(osum[:, :], osq[:, 0, :], osq[:, 1, :], ALU.add).then_inc(sem["osum_done"], 1)
        dve.memset(zp[:, :, 0:2], 0.0)
        finish(HEADS - 1)
        dve.wait_ge(sem["x_back"], 16)
        update_x(lambda m: ("w_out", m), 1)

        def convolve(src, out, w_col, bias):
            dve.tensor_scalar(out, src[:, 0:YN], w_col(0), w_col(3) if bias else None, ALU.mult,
                              ALU.add if bias else ALU.bypass)
            for j in (1, 2):
                dve.drain()
                last = dve.scalar_tensor_tensor(out=out, in0=src[:, j:j + YN], scalar=w_col(j), in1=out,
                                                op0=ALU.mult, op1=ALU.add)
            return last

        def gate_hidden(gate, f):
            up = y[:, 1, :]
            dve.tensor_tensor(hh[:, 0:PROMPT], gate[0][:, 0:PROMPT], up[:, 0:PROMPT], ALU.mult)
            dve.tensor_tensor(blocks(hh[:, PROMPT:TOK], SLEN), gate[1],
                              blocks(up[:, SB:PADDED], SW)[:, :, 0:SLEN], ALU.mult)
            dve.drain()
            dve.tensor_copy(gh[:, f, :], hh[:, :])
            dve.drain()
            dve.tensor_tensor(gl[:, f, :], hh[:, :], gh[:, f, :].bitcast(F32),
                              ALU.subtract).then_inc(sem["g_done"], 1)

        def take_padded(p, zi, factor, cut):
            if cut == HP:
                dve.tensor_tensor(zp[:, zi, 2:SB].rearrange("p (h t) -> p h t", h=2), slot(p, HP),
                                  factor[:, 0:PROMPT].rearrange("p (h t) -> p h t", h=2), ALU.mult)
            else:
                dve.tensor_tensor(zp[:, zi, 2:2 + cut], ps[:, p, 0:cut], factor[:, 0:cut], ALU.mult)
                dve.tensor_tensor(zp[:, zi, 2 + cut:SB], ps[:, p, BANK:BANK + PROMPT - cut],
                                  factor[:, cut:PROMPT], ALU.mult)
            a = BANK + PROMPT - cut
            dve.tensor_tensor(blocks(zp[:, zi, SB:PADDED], SW)[:, :, 2:SW], blocks(ps[:, p, a:a + SAMPLE], SLEN),
                              blocks(factor[:, PROMPT:TOK], SLEN), ALU.mult).then_inc(freed[p], 1)

        def z_unit(step, layer, z, j, i=0):
            zz = z + layer * ZT
            p = take(step, i)
            if not (isinstance(z, int) and zz < 4):
                dve.wait_ge(sem["zl_saved"], zz - 3)
            take_padded(p, j, rstd, HP)
            dve.drain()
            dve.wait_ge(sem["pads_in"], zz + 1)

            def col(c):
                return par[:, bass.ds(zz * 4 + (C_FFN + c), 1)]

            convolve(zp[:, j, :], y[:, j % 2, 0:YN], col, True).then_inc(sem["y_done"], 1)

        def group(layer, g, z0, i=0, f_count=None):
            for j in range(4):
                z_unit(("z", layer, g, j), layer, z0 + j, j, i)
                if j % 2:
                    dve.drain()
                    dve.wait_ge(sem["gate_silu"], f_count + (j + 1) // 2)
                    gate_hidden((sg[:, :], blocks(sg[:, SB:PADDED], SW)[:, :, 0:SLEN]), 2 * (g % 2) + j // 2)

        def down(layer, g, i=0):
            for m in range(KT):
                p = take(("down", layer, g, m), i)
                dve.tensor_tensor(two(x[:, m, :]), slot(p), two(x[:, m, :]), ALU.add).then_inc(freed[p], 1)
            dve.drain()

        def mixer():
            dve.wait_ge(sem["zl_saved"], ZT)
            for g in range(MIX_G + 1):
                if g < MIX_G:
                    for e in range(2):
                        E = 2 * g + e
                        dve.drain()
                        p = take(("mix", g, 3 * e))
                        dve.tensor_tensor(two(bg[:, e, :]), slot(p), two(rstd[:, :]),
                                          ALU.mult).then_inc(freed[p], 1)
                        p = take(("mix", g, 3 * e + 1))
                        dve.tensor_tensor(two(cg[:, :]), slot(p), two(rstd[:, :]), ALU.mult).then_inc(freed[p], 1)
                        dve.drain()
                        dve.tensor_tensor(cg[:, :], cg[:, :], rstd[:, :], ALU.mult)
                        dve.drain()
                        p = take(("mix", g, 3 * e + 2))
                        if E >= 2:
                            dve.wait_ge(sem["cl_saved"], E - 1)
                        take_padded(p, e, cg, HALF)
                        dve.drain()
                        dve.wait_ge(sem["cpads_in"], E + 1)
                        convolve(zp[:, e, :], y[:, 1, 0:YN],
                                 lambda c: par[:, C_SCW + 3 * E + c:C_SCW + 3 * E + c + 1],
                                 False).then_inc(sem["cy_done"], 1)
                        dve.drain()
                        gate_hidden((bg[:, e, :], blocks(bg[:, e, PROMPT:TOK], SLEN)), E % 4)
                if 1 <= g < MIX_G:
                    for m in range(KT):
                        p = take(("mix_out", g - 1, m))
                        dve.tensor_tensor(two(x[:, m, :]), slot(p), two(x[:, m, :]), ALU.add).then_inc(freed[p], 1)
                    dve.drain()
            update_x(lambda m: ("mix_out", MIX_G - 1, m), 3)

        for layer in range(2):
            n = 1 + 2 * layer
            if layer == 1:
                mixer()
                dve.wait_ge(sem["cl_saved"], KT)
            f0 = layer * FT
            invert_std(n)
            group(layer, 0, 0, f_count=f0)
            group(layer, 1, 4, f_count=f0 + 2)
            with dve.Fori(0, TRIPS) as i:
                for g in range(2):
                    down(layer, g, i)
                    group(layer, 2 + g, 8 * i + (8 + 4 * g), i, 4 * i + (f0 + 4 + 2 * g))
            down(layer, 8)
            group(layer, 10, 40, f_count=f0 + 20)
            down(layer, 9)
            update_x(lambda m: ("down", layer, 10, m), n + 1)
            if layer == 0:
                invert_std(2)
        invert_std(4)
        for m in range(KT):
            dve.scalar_tensor_tensor(out=x[:, m, :], in0=x[:, m, :], scalar=norm_col(4, m), in1=rstd[:, :],
                                     op0=ALU.mult, op1=ALU.mult).then_inc(sem["out_done"], 1)

    @block.scalar
    def _(act):
        eps = par[:, C_EPS:C_EPS + 1]

        def take(step, i=0):
            p, n = slots.at(step, i)
            act.wait_ge(filled[p], n + 1)
            return p

        def copied(step):
            p, n = slots.at(step)
            act.wait_ge(freed[p], n + 1)

        def split_high(n, m):
            act.activation(xh[:, m, :], x[:, m, :], ACT.Copy, scale=norm_col(n, m)).then_inc(sem["xs_hi"], 1)

        def square(n, m):
            act.activation((sq0 if n == 0 else sq)[:, m, :], x[:, m, :], ACT.Square).then_inc(sem["sq_done"], 1)

        def root(n):
            p, _ = slots.at(("norm", n))
            take(("norm", n))
            act.activation(two(rstd[:, :]), slot(p), ACT.Sqrt, bias=eps, scale=1.0 / D)
            act.drain()
            act.nop().then_inc(sem["std_done"], 1)
            act.nop().then_inc(freed[p], 1)

        def norm_inputs(steps, n):
            for m in range(KT):
                copied(steps(m))
                if n < 4:
                    split_high(n, m)
                square(n, m)

        act.dma_start(wgd_raw[:, :, :], wgd_in).then_inc(sem["gla_in"], 16)
        act.dma_start(wgu[:, :], wgu_in).then_inc(sem["gla_in"], 16)
        act.dma_start(reset[:, :], reset_in).then_inc(sem["gla_in"], 16)
        act.wait_ge(sem["par_in"], 16)
        for m in range(KT):
            act.wait_ge(x_in_s[m], 16)
            split_high(0, m)
            square(0, m)
        act.drain()
        act.wait_ge(sem["xs_lo"], KT)
        act.dma_start(mask_words[:, :], mask_in).then_inc(sem["mask_in"], 16)
        root(0)

        for h in range(HEADS):
            copied(("gate_up", h))
            act.activation(soft[:, h, :], pre[:, h, :], ACT.Abs)
        act.drain()
        act.activation(soft[:, :, :], soft[:, :, :], ACT.Exp, scale=-1.0)
        act.drain()
        act.activation(soft[:, :, :], soft[:, :, :], ACT.Ln, bias=1.0).then_inc(sem["soft_done"], 1)

        def decay(h, t):
            w = TOK if t >= 7 or LEVELS[t] < SLEN else TAIL
            e = dE[:, t % 2, 0:w]
            if t < 8:
                act.wait_ge(sem["d_done"], 8 * h + t + 1)
            if t < 7:
                act.activation(e, e, ACT.Abs)
                act.drain()
                act.activation(e, e, ACT.Exp, scale=-1.0 / TAU).then_inc(sem["e_done"], 1)
            elif t == 7:
                act.activation(e, e, ACT.Exp, scale=1.0 / TAU).then_inc(sem["e_done"], 1)
            else:
                act.wait_ge(sem["lev_done"], 9 * h + 7)
                act.activation(e, b[:, h, :], ACT.Exp, scale=1.0 / TAU).then_inc(sem["e_done"], 1)

        def v_to_tokens(h, e):
            p = take(("vT", h, e))
            c = (2 * h + e) * P
            act.copy(v_tok[:, :, c:c + P], blocks(ps[:, p, 0:6 * P], P)).then_inc(freed[p], 1)

        def gate_r(h, e):
            copied(("r", h, e))
            act.activation(sr[:, 2 * h + e, :], stage[:, e, :], ACT.Silu).then_inc(sem["r_silu"], 1)

        for h in range(HEADS):
            for t in range(4):
                decay(h, t)
            v_to_tokens(h, 0)
            decay(h, 4)
            decay(h, 5)
            v_to_tokens(h, 1)
            gate_r(h, 0)
            decay(h, 6)
            decay(h, 7)
            gate_r(h, 1)
            decay(h, 8)
            act.activation(dec[:, h, 0:4], blocks(b[:, h, 0:TAIL], CH)[:, :, CH - 1], ACT.Exp, scale=1.0 / TAU)
            act.activation(dec[:, h, 4:13], blocks(b[:, h, TAIL:TOK], SLEN)[:, :, SLEN - 1], ACT.Exp,
                           scale=1.0 / TAU).then_inc(sem["dec_done"], 1)

        def load_states(h):
            act.dma_start(s0[:, h % 2, :, :], s0_in[:, h, :, :]).then_inc(s0_in_s[h % 2], 16)

        def k_to_tokens(h):
            p = take(("kT", h))
            act.copy(kd[:, 0:5, :], blocks(ps[:, p, 0:5 * P], P))
            for odd in range(2):
                last = act.activation(kd[:, 5 + odd, :], ps[:, p, 5 * P:6 * P], ACT.Copy,
                                      scale=par[:, C_EVEN + odd:C_EVEN + odd + 1])
            last.then_inc(freed[p], 1)

        def head_root(h):
            p = take(("head_norm", h))
            act.activation(two(osq[:, 0, :]), slot(p), ACT.Sqrt, bias=eps, scale=1.0 / DV).then_inc(freed[p], 1)

        take(("r", HEADS - 1, 1))
        load_states(0)
        load_states(1)
        act.wait_ge(sem["lev_done"], 9 * HEADS)
        copied(("A", HEADS - 1, 7))
        act.drain()
        act.dma_start(x[:, :, :], x_in).then_inc(sem["x_back"], 16)
        k_to_tokens(0)
        for h in range(HEADS):
            if h:
                head_root(h - 1)
            if h + 1 < HEADS:
                k_to_tokens(h + 1)
            copied(("U", h, 3))
            act.dma_start(sp_out[:, h, :], chain[:, 4, :]).then_inc(sem["chain_stored"], 16)
            act.dma_start(ss_out[:, h, :, :], snew[:, h % 2, :, :]).then_inc(snew_stored[h % 2], 16)
            for e in range(2):
                p = take(("o", h, e))
                if e == 0 and h:
                    act.wait_ge(sem["o_done"], h)
                act.activation(osq[:, e, :], ps[:, p, 0:TOK], ACT.Square).then_inc(sem["osq_done"], 1)
            if h + 2 < HEADS:
                load_states(h + 2)
        act.dma_start(zc[:, :, :], zc_in).then_inc(sem["zc_in"], 16)
        head_root(HEADS - 1)
        act.wait_ge(sem["o_done"], HEADS)
        act.wait_ge(sem["chain_stored"], 16 * HEADS)
        for i in range(2):
            act.wait_ge(snew_stored[i], 32)
        norm_inputs(lambda m: ("w_out", m), 1)

        def pads(z, j, layer):
            zz = z + layer * ZT
            act.copy(blocks(zp[:, j, SB:PADDED], SW)[:, :, 0:2],
                     zc[:, bass.ds(zz, 1), :].rearrange("p z (s w) -> p (z s) w", w=2)
                     ).then_inc(sem["pads_in"], 1)

        def z_unit(z, j, layer, more=True):
            zz = z + layer * ZT
            act.wait_ge(sem["y_done"], zz + 1)
            act.copy(zl[:, bass.ds(zz, 1), :].rearrange("p z (s w) -> p (z s) w", w=2),
                     blocks(zp[:, j, LAST:ZW], SW)[:, :, 0:2]).then_inc(sem["zl_saved"], 1)

        def gate(f_count):
            act.wait_ge(sem["g_done"], f_count[1])
            act.activation(sg[:, 0:YN], y[:, 0, 0:YN], ACT.Silu).then_inc(sem["gate_silu"], 1)

        act.wait_ge(sem["zc_in"], 16)
        g_before = 0
        for layer in range(2):
            if layer == 1:
                norm_inputs(lambda m: ("down", 0, GROUPS - 1, m), 2)
                for e in range(2):
                    act.copy(blocks(zp[:, e, SB:PADDED], SW)[:, :, 0:2],
                             par[:, C_CCACHE + 16 * e:C_CCACHE + 16 * e + 16].rearrange("p (s w) -> p s w", w=2)
                             ).then_inc(sem["cpads_in"], 1)
                root(2)
                act.dma_start(zl_out[:, 0:ZT, :], zl[:, 0:ZT, :]).then_inc(sem["tables_out"], 16)
                for E in range(KT):
                    act.wait_ge(sem["cy_done"], E + 1)
                    act.copy(cl[:, E, :].rearrange("p (s w) -> p s w", w=2),
                             blocks(zp[:, E % 2, LAST:ZW], SW)[:, :, 0:2]).then_inc(sem["cl_saved"], 1)
                    if E + 2 < KT:
                        c = C_CCACHE + 16 * (E + 2)
                        act.copy(blocks(zp[:, E % 2, SB:PADDED], SW)[:, :, 0:2],
                                 par[:, c:c + 16].rearrange("p (s w) -> p s w", w=2)).then_inc(sem["cpads_in"], 1)
                act.drain()
                act.dma_start(cl_out, cl[:, :, :]).then_inc(sem["tables_out"], 16)
                g_before += KT
                norm_inputs(lambda m: ("mix_out", MIX_G - 1, m), 3)
            for j in range(4):
                pads(j, j, layer)
            root(1 + 2 * layer)
            with act.Fori(0, GROUPS - 1) as i:
                for j in range(4):
                    z_unit(4 * i + j, j, layer)
                    if j % 2 == 0:
                        gate((None, 2 * i + (g_before + j // 2)))
                    pads(4 * i + (4 + j), j, layer)
            for j in range(4):
                z_unit(ZT - 4 + j, j, layer)
                if j % 2 == 0:
                    gate((None, g_before + FT - 2 + j // 2))
            act.drain()
            g_before += FT
        norm_inputs(lambda m: ("down", 1, GROUPS - 1, m), 4)
        act.dma_start(zl_out[:, ZT:, :], zl[:, ZT:, :]).then_inc(sem["tables_out"], 16)
        root(4)
        act.wait_ge(sem["tables_out"], 48)

    @block.sync
    def _(sp):
        for m in range(KT):
            sp.wait_ge(sem["out_done"], m + 1)
            sp.dma_start(y_out[:, m, :], x[:, m, :]).then_inc(sem["written"], 16)
        sp.wait_ge(sem["written"], 16 * KT)

    block.__exit__(None, None, None)


def _units(w, cols):
    return [w[:, c:c + P].reshape(KT, P, P).transpose(1, 0, 2) for c in cols]


def _down_units(w, f):
    return [w[P * t:P * (t + 1), :].reshape(P, KT, P) for t in f]


def _weights(gla_w_in, gla_w_out, sc_w_in, sc_w_out, up, down):
    import numpy as np
    units = []
    for h in range(HEADS):
        units += _units(gla_w_in, [512 + P * h, P * h])
    for h in range(HEADS):
        units += _units(gla_w_in, [1024 + 256 * h, 1152 + 256 * h, 2048 + 256 * h, 2176 + 256 * h])
    units += _units(gla_w_out, [P * m for m in range(KT)])

    def ffn(layer):
        def z(g):
            return _units(up[layer], [P * f + FF * half for f in (2 * g, 2 * g + 1) for half in range(2)])

        def d(g):
            return _down_units(down[layer], (2 * g, 2 * g + 1))
        out = z(0) + z(1)
        for g in range(2, GROUPS):
            out += d(g - 2) + z(g)
        return out + d(GROUPS - 2) + d(GROUPS - 1)

    def mix_z(g):
        return _units(sc_w_in, [P * e + D * part for e in (2 * g, 2 * g + 1) for part in range(3)])

    units += ffn(0) + mix_z(0)
    for g in range(1, MIX_G):
        units += mix_z(g) + _down_units(sc_w_out, (2 * g - 2, 2 * g - 1))
    units += _down_units(sc_w_out, (2 * MIX_G - 2, 2 * MIX_G - 1)) + ffn(1)
    assert len(units) == N_UNITS
    return np.stack(units)


def _tiles(a):
    return a.T.reshape(-1, P, a.shape[0]).transpose(1, 0, 2)


def _masks():
    import numpy as np
    out = np.zeros((P, 8, TOK), np.uint8)
    for start, n in [(c * CH, CH) for c in range(NCH)] + [(TAIL, 16), (PROMPT, SAMPLE)]:
        s, t = np.arange(n)[:, None], np.arange(n)[None, :]
        out[:n, 0, start:start + n] = s == t
        for lv, m in enumerate(LEVELS):
            if m < SLEN or n == CH and start < TAIL:
                out[:n, lv + 1, start:start + n] = (s // (2 * m) == t // (2 * m)) & (s % (2 * m) < m) & (t % (2 * m) >= m)
    return out.reshape(P, -1).view(np.int32)


def kernel(**inputs):
    import numpy as np
    import concourse.bacc as bacc
    from concourse import mybir as mb
    from concourse.bass_utils import run_bass_kernel_spmd

    a = {k: np.ascontiguousarray(v) for k, v in inputs.items()}
    tokens = np.concatenate([a["meta"], a["x_prompt"][0], a["x_sample"].reshape(SAMPLE, D)])
    par = np.zeros((P, N_PAR), np.float32)
    norms = [a["norm_mix"][0], a["norm_ffn"][0], a["norm_mix"][1], a["norm_ffn"][1], a["norm_final"]]
    for n, g in enumerate(norms):
        par[:, C_NORM + 8 * n:C_NORM + 8 * n + 8] = g.reshape(KT, P).T
    par[:, C_BGATE:C_BGATE + 4] = a["gla_b_gate"][0].reshape(HEADS, P).T
    par[:, C_GAIN:C_GAIN + 8] = a["gla_head_gain"][0].reshape(KT, P).T
    par[:, C_SCW:C_SCW + 24] = a["sc_conv_w"][0].reshape(3, KT, P).transpose(2, 1, 0).reshape(P, 24)
    taps = np.concatenate([a["ffn_conv_w"], a["ffn_conv_b"][:, None, :]], axis=1)
    par[:, C_FFN:C_CCACHE] = taps.reshape(2, 4, 2, FT, P).transpose(4, 0, 3, 2, 1).reshape(P, -1)
    par[:, C_CCACHE:C_EVEN] = a["cache_conv"][0].reshape(SEQS, 2, KT, P).transpose(3, 2, 0, 1).reshape(P, -1)
    par[:, C_EVEN] = np.arange(P) // SLEN % 2 == 0
    par[:, C_ODD] = np.arange(P) // SLEN % 2
    par[:, C_EPS] = 1e-6
    wgd = a["gla_w_in"][0][:, 3072:3088].reshape(KT, P, 16).transpose(1, 0, 2)
    wgu = np.concatenate([a["gla_w_gate_up"][0]] * 2)
    reset = np.ones((P, TOK), np.float32)
    reset[:, 0:TAIL:CH] = 0
    reset[:, TAIL:TOK:SLEN] = 0
    zc = a["cache_ffn"].reshape(2, SEQS, 2, 2, FT, P).transpose(5, 0, 4, 3, 1, 2).reshape(P, 2 * ZT, 16)
    ins = {
        "x_t": _tiles(tokens), "w_units": _weights(a["gla_w_in"][0], a["gla_w_out"][0], a["sc_w_in"][0],
                                                   a["sc_w_out"][0], a["ffn_w_up"], a["ffn_w_down"]),
        "w_gate_down": wgd, "w_gate_up": wgu, "params": par, "scan_reset": reset, "level_masks": _masks(),
        "states": a["state_gla"][0].transpose(2, 1, 0, 3), "ffn_cache": zc,
    }
    outs = {"y_t": (P, KT, TOK), "state_prompt": (P, HEADS, DV), "state_sample": (P, HEADS, SEQS, DV),
            "ffn_last": (P, 2 * ZT, 18), "conv_last": (P, KT, 18)}
    nc = bacc.Bacc("TRN2", target_bir_lowering=False, num_devices=1)
    arrays, args = {}, []
    for name, v in ins.items():
        arrays[name] = np.ascontiguousarray(v)
        args.append(nc.dram_tensor(name, v.shape, mb.dt.from_np(v.dtype), kind="ExternalInput").ap())
    for name, shape in outs.items():
        args.append(nc.dram_tensor(name, shape, mb.dt.float32, kind="ExternalOutput").ap())
    build(nc, *args)
    got = run_bass_kernel_spmd(nc, [arrays], core_ids=[0]).results[0]

    y = got["y_t"].transpose(2, 1, 0).reshape(TOK, D)
    ffn = got["ffn_last"].reshape(P, 2, FT, 2, 1 + SEQS, 2).transpose(1, 4, 5, 3, 2, 0)
    ffn = ffn.reshape(2, 1 + SEQS, 2, 2 * FF)
    conv = got["conv_last"].reshape(P, KT, 1 + SEQS, 2).transpose(2, 3, 1, 0).reshape(1, 1 + SEQS, 2, D)
    c = np.ascontiguousarray
    return (c(y[16:PROMPT][None]), c(y[PROMPT:].reshape(SEQS, SLEN, D)),
            c(got["state_prompt"].transpose(1, 0, 2)[None, None]),
            c(got["state_sample"].transpose(2, 1, 0, 3)[None]),
            c(conv[:, :1]), c(conv[:, 1:]), c(ffn[:, :1]), c(ffn[:, 1:]))
```

```python
import concourse.bass as bass
from concourse import mybir

F32 = mybir.dt.float32
F32R = mybir.dt.float32r
U8 = mybir.dt.uint8
I32 = mybir.dt.int32
ALU = mybir.AluOpType
ACT = mybir.ActivationFunctionType
AX = mybir.AxisListType

P = 128
D = 1024
KT = D // P
PROMPT = 16 + 512
SEQS, SLEN = 8, 16
SAMPLE = SEQS * SLEN
TOK = PROMPT + SAMPLE
HALF = TOK // 2
HP = PROMPT // 2
HEADS, DV = 4, 256
CH = 128
NCH = PROMPT // CH
TAIL = NCH * CH
FF = 2816
FT = FF // P
ZT = 2 * FT
PADDED = 2 + PROMPT + SEQS * (2 + SLEN)
SB = 2 + PROMPT
SW = 2 + SLEN
YN = PADDED - 2
LAST = PROMPT
ZW = LAST + (1 + SEQS) * SW
BANK = 512
RING = 4
TAU = 16.0
LEVELS = [1, 2, 4, 8, 16, 32, 64]
N_UNITS = 2 * HEADS + 16 + 8 + 2 * (ZT + FT) + 24 + 8
GROUPS = FT // 2
TRIPS = (GROUPS - 3) // 2
RING_TURNS = 3
POOL_OUT = 3
MIX_G = 4

C_NORM, C_BGATE, C_GAIN = 0, 40, 44
C_SCW, C_FFN = 52, 76
C_CCACHE = C_FFN + 2 * ZT * 4
C_EVEN = C_CCACHE + KT * 16
C_ODD, C_EPS, C_HALF_EPS = C_EVEN + 1, C_EVEN + 2, C_EVEN + 3
N_PAR = C_EVEN + 4
EPS = 1e-6
ROOT_ORDER = [("norm", 0)] + [("head_norm", h) for h in range(HEADS)] + [("norm", n) for n in range(1, 4)] + [("last_norm", c) for c in range(2)]


class SlotPlan:

    def __init__(self):
        self.used = [0] * RING
        self.next = 0
        self.steps = {}

    def straight(self, *names):
        for name in names:
            p = self.next % RING
            self.steps[name] = (p, self.used[p], 0)
            self.used[p] += 1
            self.next += 1

    def loop(self, names, trips):
        per = [0] * RING
        where = [(self.next + j) % RING for j in range(len(names))]
        for p in where:
            per[p] += 1
        seen = [0] * RING
        for name, p in zip(names, where):
            self.steps[name] = (p, self.used[p] + seen[p], per[p])
            seen[p] += 1
        for p in range(RING):
            self.used[p] += trips * per[p]
        self.next += len(names)

    def at(self, name, i=0):
        p, base, per = self.steps[name]
        return p, (base + per * i if per else base)


def plan_slots():
    s = SlotPlan()
    s.straight(("k", 0), ("q", 0), ("norm", 0), "gate_down")
    s.straight(*[("gate_up", h) for h in range(HEADS)])
    for h in range(1, HEADS):
        s.straight(("k", h), ("q", h))
    for h in range(HEADS):
        s.straight(("v", h, 0), ("A", h, 0), ("A", h, 1), ("v", h, 1), ("vT", h, 0), ("A", h, 2),
                   ("A", h, 3), ("r", h, 0), ("vT", h, 1))
        if h == HEADS - 1:
            s.straight(("kT", 0))
        s.straight(("A", h, 4), ("A", h, 5), ("r", h, 1), ("A", h, 6), ("A", h, 7))
    for h in range(HEADS):
        s.straight(*[("U", h, j) for j in range(4)])
        if h:
            s.straight(("head_norm", h - 1))
        if h + 1 < HEADS:
            s.straight(("kT", h + 1))
        s.straight(("o", h, 0), ("o", h, 1))
    s.straight(("w_out", 0), ("head_norm", HEADS - 1), *[("w_out", m) for m in range(1, KT)])
    for layer in range(2):
        if layer == 1:
            for g in range(MIX_G):
                for j in range(6):
                    s.straight(("mix", g, j))
                    if g == 0 and j == 1:
                        s.straight(("norm", 2))
                if g:
                    s.straight(*[("mix_out", g - 1, m) for m in range(KT)])
            s.straight(*[("mix_out", MIX_G - 1, m) for m in range(KT)])
        s.straight(("z", layer, 0, 0), ("z", layer, 0, 1), ("norm", 1 + 2 * layer),
                   ("z", layer, 0, 2), ("z", layer, 0, 3))
        s.straight(*[("z", layer, 1, j) for j in range(4)])
        body = []
        for g in range(2):
            body += [("down", layer, g, m) for m in range(KT)] + [("z", layer, 2 + g, j) for j in range(4)]
        s.loop(body, TRIPS)
        s.straight(*[("down", layer, 8, m) for m in range(KT)])
        s.straight(*[("z", layer, 10, j) for j in range(4)])
        s.straight(*[("down", layer, 9, m) for m in range(KT)])
        if layer == 0:
            s.straight(*[("down", layer, 10, m) for m in range(KT)])
    s.straight(*[("last", 0, m) for m in range(KT)], *[("last", 1, m) for m in range(KT - 1)], ("last_norm", 0),
               ("last", 1, KT - 1), ("last_norm", 1))
    return s


def build(nc, x_in, w_in, wgd_in, wgu_in, par_in, reset_in, mask_in, s0_in, zc_in,
          y_out, sp_out, ss_out, zl_out, cl_out):
    slots = plan_slots()

    base = (nc.sbuf_base + 31) // 32 * 32
    at = [base]

    def sb(name, shape, dt=F32, offset=None, size=None):
        if offset is not None:
            return nc.alloc_sbuf_tensor_at(name, shape, dt, offset=offset)
        n = 4
        for d in shape[1:]:
            n *= d
        t = nc.alloc_sbuf_tensor_at(name, shape, dt, offset=at[0])
        at[0] += (n + 31) // 32 * 32
        return t

    T4 = 4 * TOK
    x_at = at[0]
    x = sb("x", [P, KT, TOK])
    xh_at = at[0]
    xh = sb("xh", [P, KT, TOK], F32R)
    xl = sb("xl", [P, KT, TOK], F32R)
    raw = sb("raw", [P, RING, 8, P])
    wh = sb("wh", [P, RING, 8, P], F32R)
    wl = sb("wl", [P, RING, 8, P], F32R)
    par = sb("par", [P, N_PAR])
    rstd = sb("rstd", [P, TOK])
    ones = sb("ones", [P, P])
    tiny = sb("tiny", [P, 1])
    ident = sb("ident", [P, P])
    qk_at = at[0]
    qk = sb("qk", [P, 2 * HEADS, TOK])
    sr_at = at[0]
    sr = sb("sr", [P, KT, TOK])
    b_at = at[0]
    b = sb("b", [P, HEADS, TOK])
    vt_at = at[0]
    v_tok = sb("v_tok", [P, 6, D])
    AT_at = at[0]
    AT = sb("AT", [P, HEADS, TOK])
    spare = at[0]
    osq = sb("osq", [P, 2, TOK])
    dec = sb("dec", [P, HEADS, 13])
    gla_end = at[0]
    reset = sb("reset", [P, TOK], offset=AT_at)
    gd = sb("gd", [32, TOK], offset=AT_at + T4)
    wgu = sb("wgu", [32, 512], offset=AT_at + 2 * T4)
    wgd_raw = sb("wgd_raw", [P, KT, 16], offset=AT_at + 2 * T4 + 2048)
    wgd = sb("wgd", [P, KT, 32], F32R, offset=AT_at + 2 * T4 + 2560)
    pre = sb("pre", [P, HEADS, TOK], offset=sr_at)
    soft = sb("soft", [P, HEADS, TOK], offset=sr_at + 4 * T4)
    sq0 = sb("sq0", [P, KT, TOK], offset=b_at)
    lev = sb("lev", [P, 2, TOK], offset=x_at)
    dE = sb("dE", [P, 2, TOK], offset=x_at + 2 * T4)
    stage = sb("stage", [P, 2, TOK], offset=x_at + 4 * T4)
    mask_words = sb("mask", [P, 8 * TOK // 4], I32, offset=x_at + 6 * T4)
    mask = mask_words[:, :].bitcast(U8).rearrange("p (l t) -> p l t", l=8)
    s0 = sb("s0", [P, 2, SEQS, DV], offset=xh_at)
    snew = sb("snew", [P, 2, SEQS, DV], offset=xh_at + 16384)
    o32 = sb("o32", [P, 2, TOK], offset=xh_at + 32768)
    osum = sb("osum", [P, TOK], offset=xh_at + 32768 + 2 * T4)
    kd = sb("kd", [P, 7, P], offset=b_at)
    chain = sb("chain", [P, 5, DV], offset=b_at + 3584)
    head_std = AT[:, 0, :]
    oh = sb("oh", [P, KT, TOK], F32R, offset=sr_at)
    ol = sb("ol", [P, KT, TOK], F32R, offset=qk_at)
    at[0] = qk_at
    gh = sb("gh", [P, 4, TOK], F32R)
    gl = sb("gl", [P, 4, TOK], F32R)
    assert at[0] <= sr_at
    at[0] = sr_at
    y = sb("y", [P, 2, PADDED])
    sg = sb("sg", [P, PADDED])
    hh = sb("hh", [P, TOK])
    cg = sb("cg", [P, TOK])
    bg = sb("bg", [P, 2, TOK])
    assert at[0] <= b_at
    at[0] = b_at
    sq = sb("sq", [P, KT, TOK])
    zc = sb("zc", [P, 2 * ZT, 16])
    zl = sb("zl", [P, 2 * ZT, 18])
    cl = sb("cl", [P, KT, 18])
    zp = sb("zp", [P, 4, ZW])
    at[0] = max(at[0], gla_end)
    assert at[0] <= nc.sbuf_top

    ps = nc.alloc_psum_tensor("ps", [P, RING, 2 * BANK], F32)

    names = ["par_in", "gla_in", "wgd_done", "hi_done", "lo_done", "units_used", "consts",
             "xs_hi", "xs_lo", "sq_done", "sum_done", "log_done", "root_done", "soft_done", "mask_in", "d_done", "e_done",
             "lev_done", "r_silu", "dec_done", "chain_stored", "osq_done", "osum_done", "o_done", "o_scaled", "oh_done", "x_back",
             "zc_in", "pads_in", "y_done", "zl_saved", "gate_silu", "g_done", "cpads_in", "cy_done",
             "cl_saved", "out_done", "pool_out", "gained", "final_std", "written", "tables_out"]
    sem = {n: nc.alloc_semaphore(n) for n in names}
    filled = [nc.alloc_semaphore(f"filled{i}") for i in range(RING)]
    freed = [nc.alloc_semaphore(f"freed{i}") for i in range(RING)]
    landed = [nc.alloc_semaphore(f"landed{i}") for i in range(RING)]
    x_in_s = [nc.alloc_semaphore(f"x_in{i}") for i in range(KT)]
    snew_stored = [nc.alloc_semaphore(f"snew_stored{i}") for i in range(2)]
    s0_in_s = [nc.alloc_semaphore(f"s0_in{i}") for i in range(2)]

    def two(ap):
        return ap.rearrange("p (h t) -> p h t", h=2)

    def slot(p, n=HALF):
        return ps[:, p, :].rearrange("p (h t) -> p h t", h=2)[:, :, 0:n]

    def blocks(ap, n):
        return ap.rearrange("p (n t) -> p n t", t=n)

    def later(ap, m):
        return blocks(ap, 2 * m)[:, :, m:2 * m]

    def half(c):
        return slice(c * HALF, (c + 1) * HALF)

    def bank(p, c):
        return ps[:, p, c * BANK:c * BANK + HALF]

    def norm_col(n, m):
        return par[:, C_NORM + 8 * n + m:C_NORM + 8 * n + m + 1]

    block = nc.Block()
    block.__enter__()

    @block.sync
    def _(sp):
        sp.dma_start(raw[:, 0, :, :], w_in[0]).then_inc(landed[0], 16)
        sp.dma_start(par[:, :], par_in).then_inc(sem["par_in"], 16)
        for k in range(KT):
            sp.dma_start(x[:, k, :], x_in[:, k, :]).then_inc(x_in_s[k], 16)
            if k == KT // 2 - 1:
                sp.dma_start(raw[:, 1, :, :], w_in[1]).then_inc(landed[1], 16)
        for j in (2, 3):
            sp.dma_start(raw[:, j, :, :], w_in[j]).then_inc(landed[j], 16)
        with sp.Fori(0, N_UNITS // RING - 1) as i:
            for j in range(RING):
                sp.wait_ge(sem["lo_done"], RING * i + j + 1)
                sp.dma_start(raw[:, j, :, :], w_in[bass.ds(RING * i + (RING + j), 1)]
                             .rearrange("u p m n -> p (u m) n")).then_inc(landed[j], 16)

    @block.gpsimd
    def _(pool):
        pool.memset(ones[:, :], 1.0)
        pool.memset(ident[:, :], 0.0)
        pool.drain()
        pool.affine_select(out=ident[:, :], in_=ident[:, :], compare_op=ALU.not_equal, fill=1.0, base=0,
                           pattern=[[-1, P]], channel_multiplier=1).then_inc(sem["consts"], 1)

        def low(j, done):
            pool.wait_ge(sem["hi_done"], done)
            pool.tensor_tensor(wl[:, j, :, :], raw[:, j, :, :], wh[:, j, :, :].bitcast(F32),
                               ALU.subtract).then_inc(sem["lo_done"], 1)

        pool.wait_ge(sem["lo_done"], 1)
        for j in range(1, RING):
            low(j, j + 1)
        before_out = 2 * HEADS // RING + 4
        with pool.Fori(0, before_out) as i:
            for j in range(RING):
                low(j, RING * i + (RING + j + 1))
        for k in range(KT):
            pool.wait_ge(sem["oh_done"], k + 1)
            pool.tensor_tensor(ol[:, k, :], qk[:, k, :], oh[:, k, :].bitcast(F32),
                               ALU.subtract).then_inc(sem["o_done"], 1)
        with pool.Fori(0, N_UNITS // RING - 1 - before_out) as i:
            for j in range(RING):
                low(j, RING * i + (RING * (1 + before_out) + j + 1))
        for c in range(2):
            pool.wait_ge(sem["gained"], POOL_OUT * (c + 1))
            pool.wait_ge(sem["final_std"], c + 1)
            for m in range(KT - POOL_OUT, KT):
                pool.tensor_tensor(x[:, m, half(c)], x[:, m, half(c)], rstd[:, half(c)],
                                   ALU.mult).then_inc(sem["pool_out"], 1)

    @block.tensor
    def _(pe):
        unit = [0]

        def open_slot(step, i=0):
            p, n = slots.at(step, i)
            if not (isinstance(n, int) and n == 0):
                pe.wait_ge(freed[p], n)
            return p

        def copied(step):
            p, n = slots.at(step)
            pe.wait_ge(freed[p], n + 1)

        def weights(n_ready):
            pe.wait_ge(sem["lo_done"], n_ready)

        def project(step, hi, lo, n_ready, ring, cut, i=0, release=1, before=None):
            p = open_slot(step, i)
            weights(n_ready)
            halves = ((0, 0, cut), (BANK, cut, TOK))
            for k in range(KT):
                if before:
                    before(k)
                for w, v in ((wh, hi), (wh, lo), (wl, hi)):
                    for c, a, z in halves:
                        first = k == 0 and w is wh and v is hi
                        mm = pe.matmul(ps[:, p, c:c + z - a], w[:, ring, k, :], v[:, k, a:z], start=first,
                                       stop=(k == KT - 1 and w is wl))
                        if k == 0 and w is wh and v is hi and c and release:
                            mm.then_inc(sem["units_used"], release)
            mm.then_inc(filled[p], 1)

        def project_down(step, f0, n_ready, rings, i=0, release=1, g_count=None):
            weights(n_ready)
            pe.wait_ge(sem["g_done"], g_count)
            for m in range(KT):
                p = open_slot(step(m), i)
                for f in range(2):
                    for w, v in ((wh, gh), (wh, gl), (wl, gh)):
                        for c, a in ((0, 0), (BANK, HALF)):
                            mm = pe.matmul(ps[:, p, c:c + HALF], w[:, rings[f], m, :], v[:, f0 + f, a:a + HALF],
                                           start=(f == 0 and w is wh and v is gh), stop=(f == 1 and w is wl))
                            if m == 0 and f == 0 and w is wh and v is gh and c:
                                mm.then_inc(sem["units_used"], release)
                mm.then_inc(filled[p], 1)

        def norm_sum(n):
            p = open_slot(("norm", n))
            pe.wait_ge(sem["sum_done"], n + 1)
            src = sq0 if n == 0 else sq
            for c, a in ((0, 0), (BANK, HALF)):
                mm = pe.matmul(ps[:, p, c:c + HALF], ones[:, :], src[:, 0, a:a + HALF], start=True, stop=True)
            mm.then_inc(filled[p], 1)

        n_unit = 0

        def x_ready(n):
            return lambda k: pe.wait_ge(sem["xs_lo"], KT * n + k + 1)

        def norm_amid(n):
            return lambda k: norm_sum(n) if k == KT // 2 else None

        pe.wait_ge(sem["consts"], 1)
        for h in range(HEADS):
            for j, kind in enumerate("kq"):
                project((kind, h), xh, xl, n_unit + 1, n_unit % RING, HALF, release=1 if n_unit else 0,
                        before=(x_ready(0), norm_amid(0))[j] if h == 0 else None)
                n_unit += 1
            if h == 0:
                p = open_slot("gate_down")
                pe.wait_ge(sem["wgd_done"], 1)
                for k in range(KT):
                    for v in (xh, xl):
                        for c, a in ((0, 0), (BANK, HALF)):
                            mm = pe.matmul(ps[0:32, p, c:c + HALF], wgd[:, k, :], v[:, k, a:a + HALF],
                                           start=(k == 0 and v is xh), stop=(k == KT - 1 and v is xl))
                mm.then_inc(filled[p], 1)
                copied("gate_down")
                pe.wait_ge(sem["gla_in"], 48)
                for g in range(HEADS):
                    p = open_slot(("gate_up", g))
                    for c, a in ((0, 0), (BANK, HALF)):
                        mm = pe.matmul(ps[:, p, c:c + HALF], wgu[:, g * P:(g + 1) * P], gd[:, a:a + HALF],
                                       start=True, stop=True)
                    mm.then_inc(filled[p], 1)

        def scores(h, lv):
            p = open_slot(("A", h, lv))
            if lv == 0:
                ks, qs = qk[:, 2 * h, :], qk[:, 2 * h + 1, :]
                copied(("k", h))
                copied(("q", h))
            else:
                ks = qs = lev[:, (lv - 1) % 2, :]
                pe.wait_ge(sem["lev_done"], 9 * h + lv)
            def queries(ap, a, z):
                return later(ap[:, a:z], LEVELS[lv - 1]) if lv else ap[:, a:z]

            def product(a, z):
                return pe.matmul(queries(ps[:, p, :], a, z), ks[:, a:a + P], queries(qs, a, z), start=True, stop=True)

            for c in range(NCH):
                mm = product(c * CH, (c + 1) * CH)
            if lv == 0 or LEVELS[lv - 1] < SLEN:
                product(TAIL, PROMPT)
                mm = product(PROMPT, TOK)
            mm.then_inc(filled[p], 1)

        starts = [c * CH for c in range(NCH)] + [TAIL, PROMPT]

        def to_tokens(step, src):
            p = open_slot(step)
            for t, a in enumerate(starts):
                mm = pe.transpose(ps[:, p, t * P:(t + 1) * P], src[:, a:a + P], ident[:, :])
            mm.then_inc(filled[p], 1)

        def value(kind, h, e):
            nonlocal n_unit
            project((kind, h, e), xh, xl, n_unit + 1, n_unit % RING, HALF)
            n_unit += 1

        def transpose_v(h, e):
            copied(("v", h, e))
            to_tokens(("vT", h, e), stage[:, e, :])

        def transpose_k(h):
            pe.wait_ge(sem["lev_done"], 9 * h + 8)
            to_tokens(("kT", h), qk[:, 2 * h, :])

        for h in range(HEADS):
            value("v", h, 0)
            scores(h, 0)
            scores(h, 1)
            value("v", h, 1)
            transpose_v(h, 0)
            scores(h, 2)
            scores(h, 3)
            value("r", h, 0)
            transpose_v(h, 1)
            if h == HEADS - 1:
                transpose_k(0)
            scores(h, 4)
            scores(h, 5)
            value("r", h, 1)
            scores(h, 6)
            scores(h, 7)

        def update(h, j, n, lhsT, rhs):
            p, _ = slots.at(("U", h, j))
            return pe.matmul(ps[:, p, n * DV:(n + 1) * DV], lhsT, rhs, start=True, stop=True,
                             skip_group_check=True), p

        def head_norm(h):
            p = open_slot(("head_norm", h))
            pe.wait_ge(sem["osum_done"], h + 1)
            for c, a in ((0, 0), (BANK, HALF)):
                mm = pe.matmul(ps[:, p, c:c + HALF], ones[:, :], osum[:, a:a + HALF], start=True, stop=True)
            mm.then_inc(filled[p], 1)

        for h in range(HEADS):
            vs = slice(h * DV, (h + 1) * DV)
            copied(("kT", h))
            for e in range(2):
                copied(("vT", h, e))
            open_slot(("U", h, 0))
            for c in range(NCH):
                mm, p = update(h, 0, c, kd[:, c, :], v_tok[:, c, vs])
                if h == c == 0:
                    mm.then_inc(sem["units_used"], 1)
            mm.then_inc(filled[p], 1)
            for j in (1, 2):
                open_slot(("U", h, j))
                for n in range(4):
                    s = 4 * (j - 1) + n
                    rows = slice(32 * (s // 2), 32 * (s // 2) + 32)
                    mm, p = update(h, j, n, kd[rows, 5 + s % 2, :], v_tok[rows, 5, vs])
                mm.then_inc(filled[p], 1)
            open_slot(("U", h, 3))
            mm, p = update(h, 3, 0, kd[0:16, 4, :], v_tok[0:16, 4, vs])
            mm.then_inc(filled[p], 1)
            if h:
                head_norm(h - 1)
            if h + 1 < HEADS:
                transpose_k(h + 1)
            copied(("U", h, 0))
            pe.wait_ge(s0_in_s[h % 2], 16 * (h // 2 + 1))
            pe.wait_ge(sem["lev_done"], 9 * h + 9)
            copied(("A", h, 7))
            q = qk[:, 2 * h + 1, :]
            for e in range(2):
                p = open_slot(("o", h, e))
                es = slice(h * DV + e * P, h * DV + (e + 1) * P)
                ee = slice(e * P, (e + 1) * P)

                def mm_o(a, z, lhsT, rhs, start, stop):
                    return pe.matmul(ps[:, p, a:z], lhsT, rhs, start=start, stop=stop, skip_group_check=True)

                for c in range(NCH):
                    a, z = c * CH, (c + 1) * CH
                    mm_o(a, z, v_tok[:, c, es], AT[:, h, a:z], True, c == 0)
                    if c:
                        mm_o(a, z, chain[:, c - 1, ee], q[:, a:z], False, True)
                mm_o(TAIL, PROMPT, v_tok[0:16, 4, es], AT[0:16, h, TAIL:PROMPT], True, False)
                mm_o(TAIL, PROMPT, chain[:, 3, ee], q[:, TAIL:PROMPT], False, True)
                mm_o(PROMPT, TOK, v_tok[:, 5, es], AT[:, h, PROMPT:TOK], True, False)
                for s in range(SEQS):
                    a = PROMPT + s * SLEN
                    mm = mm_o(a, a + SLEN, s0[:, h % 2, s, ee], q[:, a:a + SLEN], False, s == SEQS - 1)
                mm.then_inc(filled[p], 1)
        EARLY = 3
        for m in range(EARLY):
            p = open_slot(("w_out", m))
            weights(n_unit + m + 1)
            for k in range(KT - 2):
                if m == 0:
                    pe.wait_ge(sem["o_done"], k + 1)
                for w, v in ((wh, oh), (wh, ol), (wl, oh)):
                    for c, a in ((0, 0), (BANK, HALF)):
                        pe.matmul(ps[:, p, c:c + HALF], w[:, (n_unit + m) % RING, k, :], v[:, k, a:a + HALF],
                                  start=(k == 0 and w is wh and v is oh), stop=False)
            if m == 0:
                head_norm(HEADS - 1)
        for m in range(EARLY):
            p, _ = slots.at(("w_out", m))
            for k in (KT - 2, KT - 1):
                pe.wait_ge(sem["o_done"], k + 1)
                for w, v in ((wh, oh), (wh, ol), (wl, oh)):
                    for c, a in ((0, 0), (BANK, HALF)):
                        mm = pe.matmul(ps[:, p, c:c + HALF], w[:, (n_unit + m) % RING, k, :], v[:, k, a:a + HALF],
                                       start=False, stop=(k == KT - 1 and w is wl))
                        if m and k == KT - 2 and c and w is wh and v is oh:
                            mm.then_inc(sem["units_used"], 1)
            mm.then_inc(filled[p], 1)
        n_unit += EARLY
        for m in range(EARLY, KT):
            project(("w_out", m), oh, ol, n_unit + 1, n_unit % RING, HALF)
            n_unit += 1

        g_before = 0
        for layer in range(2):
            if layer == 1:
                for g in range(MIX_G):
                    for j in range(6):
                        project(("mix", g, j), xh, xl, n_unit + 1, n_unit % RING, HALF,
                                release=2 if j == 0 and (g != 1) else 1,
                                before=(x_ready(2), norm_amid(2))[j] if g == 0 and j < 2 else None)
                        n_unit += 1
                    if g:
                        project_down(lambda m, g=g: ("mix_out", g - 1, m), 2 * ((g - 1) % 2), n_unit + 2,
                                     [n_unit % RING, (n_unit + 1) % RING], g_count=g_before + 2 * g)
                        n_unit += 2
                project_down(lambda m: ("mix_out", MIX_G - 1, m), 2 * ((MIX_G - 1) % 2), n_unit + 2,
                             [n_unit % RING, (n_unit + 1) % RING], release=2, g_count=g_before + 2 * MIX_G)
                n_unit += 2
                g_before += 2 * MIX_G
            def z_units(g, i=0, release=1, norm=None):
                nonlocal n_unit
                for j in range(4):
                    u = n_unit + j
                    project(("z", layer, g, j), xh, xl, 12 * i + (u + 1), u % RING, HP, i=i,
                            release=release if j == 0 else 1,
                            before=(x_ready(norm), norm_amid(norm))[j] if norm is not None and j < 2 else None)
                n_unit += 4

            def down_units(g, count, i=0, release=1):
                nonlocal n_unit
                u = n_unit
                project_down(lambda m: ("down", layer, g, m), 2 * (g % 2), 12 * i + (u + 2),
                             [u % RING, (u + 1) % RING], i=i, release=release, g_count=count)
                n_unit += 2

            z_units(0, release=2 if layer else 1, norm=1 + 2 * layer)
            z_units(1)
            with nc.Fori(0, TRIPS, engines=[mybir.EngineType.PE], hint_back_edge=True) as i:
                for g in range(2):
                    down_units(g, 4 * i + (g_before + 2 * g + 2), i=i)
                    z_units(2 + g, i=i, release=2)
            n_unit += 12 * (TRIPS - 1)
            down_units(8, g_before + 18)
            z_units(10, release=2)
            down_units(9, g_before + 20)
            if layer == 0:
                down_units(10, g_before + 22, release=2)
            g_before += FT

        def last_norm(c):
            p = open_slot(("last_norm", c))
            pe.wait_ge(sem["sum_done"], 5 + c)
            pe.matmul(bank(p, c), ones[:, :], sq[:, 0, half(c)], start=True, stop=True).then_inc(filled[p], 1)

        weights(N_UNITS)
        pe.wait_ge(sem["g_done"], g_before)
        for c in range(2):
            for m in range(KT):
                p = open_slot(("last", c, m))
                for f in range(2):
                    for w, v in ((wh, gh), (wh, gl), (wl, gh)):
                        mm = pe.matmul(bank(p, c), w[:, (n_unit + f) % RING, m, :], v[:, f, half(c)],
                                       start=(f == 0 and w is wh and v is gh), stop=(f == 1 and w is wl))
                mm.then_inc(filled[p], 1)
                if c and m == KT - 2:
                    last_norm(0)
        last_norm(1)
        n_unit += 2
        assert n_unit == N_UNITS

    @block.vector
    def _(dve):
        def take(step, i=0):
            p, n = slots.at(step, i)
            dve.wait_ge(filled[p], n + 1)
            return p

        def split_low(n, m):
            dve.wait_ge(sem["xs_hi"], KT * n + m + 1)
            dve.scalar_tensor_tensor(out=xl[:, m, :], in0=x[:, m, :], scalar=norm_col(n, m),
                                     in1=xh[:, m, :].bitcast(F32), op0=ALU.mult,
                                     op1=ALU.subtract).then_inc(sem["xs_lo"], 1)

        def add_square(n, m):
            if m == 0:
                return
            dve.wait_ge(sem["sq_done"], KT * n + m + 1)
            if m > 1:
                dve.drain()
            total, src = (sq0 if n == 0 else sq)[:, 0, :], (sq0 if n == 0 else sq)[:, m, :]
            ins = dve.tensor_tensor(total, total, src, ALU.add)
            if m == KT - 1:
                ins.then_inc(sem["sum_done"], 1)

        def half_square(n_root, step, v, d, c=None):
            p = take(step)
            dve.wait_ge(sem["log_done"], n_root + 1)
            out, src = (two(v), slot(p)) if c is None else (v, bank(p, c))
            dve.tensor_scalar(out, src, -0.5 / d, par[:, C_HALF_EPS:C_HALF_EPS + 1], ALU.mult,
                              ALU.add).then_inc(freed[p], 1)

        def refine(n_root, r, v):
            dve.wait_ge(sem["root_done"], n_root + 1)
            dve.drain()
            dve.tensor_tensor(v, v, r, ALU.mult)
            dve.drain()
            dve.tensor_tensor(v, v, r, ALU.mult)
            dve.drain()
            dve.scalar_tensor_tensor(out=r, in0=v, scalar=1.5, in1=r, op0=ALU.add, op1=ALU.mult)
            dve.drain()

        def inverse_root(step, r, v, d):
            half_square(ROOT_ORDER.index(step), step, v, d)
            refine(ROOT_ORDER.index(step), r, v)

        def invert_std(n):
            inverse_root(("norm", n), rstd[:, :], osq[:, 1, :] if n == 0 else cg[:, :], D)

        def update_x(steps, n):
            for m in range(KT):
                p = take(steps(m))
                dve.tensor_tensor(two(x[:, m, :]), slot(p), two(x[:, m, :]), ALU.add).then_inc(freed[p], 1)
                if m:
                    split_low(n, m - 1)
                    if n == 1:
                        add_square(n, m - 1)
            split_low(n, KT - 1)
            for m in [KT - 1] if n == 1 else range(KT):
                add_square(n, m)

        dve.wait_ge(sem["hi_done"], 1)
        dve.tensor_tensor(wl[:, 0, :, :], raw[:, 0, :, :], wh[:, 0, :, :].bitcast(F32),
                          ALU.subtract).then_inc(sem["lo_done"], 1)

        dve.wait_ge(sem["par_in"], 16)
        for m in range(KT):
            split_low(0, m)
            if 2 <= m:
                add_square(0, m - 2)
        for m in range(KT - 2, KT):
            add_square(0, m)
        dve.wait_ge(sem["gla_in"], 48)
        dve.tensor_copy(wgd[:, :, 0:16], wgd_raw[:, :, :])
        dve.drain()
        dve.tensor_tensor(wgd[:, :, 16:32], wgd_raw[:, :, :], wgd[:, :, 0:16].bitcast(F32),
                          ALU.subtract).then_inc(sem["wgd_done"], 1)
        invert_std(0)

        def take_kq(h):
            p = take(("k", h))
            dve.tensor_tensor(two(qk[:, 2 * h, :]), slot(p), two(rstd[:, :]), ALU.mult).then_inc(freed[p], 1)
            p = take(("q", h))
            dve.scalar_tensor_tensor(out=two(qk[:, 2 * h + 1, :]), in0=slot(p), scalar=float(P) ** -0.5,
                                     in1=two(rstd[:, :]), op0=ALU.mult, op1=ALU.mult).then_inc(freed[p], 1)

        take_kq(0)
        p = take("gate_down")
        dve.tensor_tensor(two(gd[:, :]), slot(p)[0:32], two(rstd[0:32, :]), ALU.mult).then_inc(freed[p], 1)
        for h in range(HEADS):
            p = take(("gate_up", h))
            dve.tensor_scalar(two(pre[:, h, :]), slot(p), par[:, C_BGATE + h:C_BGATE + h + 1], None,
                              ALU.add).then_inc(freed[p], 1)
        take_kq(1)
        dve.wait_ge(sem["soft_done"], 1)
        dve.scalar_tensor_tensor(out=pre[:, :, :], in0=pre[:, :, :], scalar=0.0, in1=soft[:, :, :],
                                 op0=ALU.min, op1=ALU.subtract)
        dve.drain()
        for h in range(HEADS):
            dve.tensor_tensor_scan(b[:, h, :], reset[:, :], pre[:, h, :], 0.0, ALU.mult, ALU.add)
        dve.drain()
        take_kq(2)
        take_kq(3)

        def width(t):
            return TOK if LEVELS[t] < SLEN else TAIL

        def distance(h, t):
            if t < 7:
                m, w = LEVELS[t], width(t)
                bb = blocks(b[:, h, 0:w], 2 * m)
                ref = bb[:, :, m - 1:m].to_broadcast([P, w // (2 * m), 2 * m])
                dve.tensor_tensor(blocks(dE[:, t % 2, 0:w], 2 * m), bb, ref,
                                  ALU.subtract).then_inc(sem["d_done"], 1)
                return
            for a, z, m in ((0, TAIL, CH), (TAIL, TOK, SLEN)):
                bb = blocks(b[:, h, a:z], m)
                ref = bb[:, :, m - 1:m].to_broadcast([P, (z - a) // m, m])
                last = dve.tensor_tensor(blocks(dE[:, t % 2, a:z], m), ref, bb, ALU.subtract)
            last.then_inc(sem["d_done"], 1)

        def decayed(h, t):
            dve.wait_ge(sem["e_done"], 9 * h + t + 1)
            k, q = qk[:, 2 * h, :], qk[:, 2 * h + 1, :]
            if t < 7:
                m, w = LEVELS[t], width(t)
                for src, part in ((k, slice(0, m)), (q, slice(m, 2 * m))):
                    last = dve.tensor_tensor(blocks(lev[:, t % 2, 0:w], 2 * m)[:, :, part],
                                             blocks(dE[:, t % 2, 0:w], 2 * m)[:, :, part],
                                             blocks(src[:, 0:w], 2 * m)[:, :, part], ALU.mult)
            else:
                src = k if t == 7 else q
                last = dve.tensor_tensor(src, src, dE[:, t % 2, :], ALU.mult)
            last.then_inc(sem["lev_done"], 1)

        def keep(h, lv):
            p = take(("A", h, lv))
            if lv == 0:
                out, m, src = AT[:, h, :], mask[:, 0, :], ps[:, p, 0:TOK]
            else:
                out, m, src = (later(a[:, 0:width(lv - 1)], LEVELS[lv - 1])
                               for a in (AT[:, h, :], mask[:, lv, :], ps[:, p, :]))
            dve.copy_predicated(out, m, src).then_inc(freed[p], 1)

        def take_value(kind, h, e):
            if kind == "v" and h:
                dve.wait_ge(sem["r_silu"], 2 * (h - 1) + e + 1)
            if kind == "r":
                take(("vT", h, e))
            p = take((kind, h, e))
            dve.tensor_tensor(two(stage[:, e, :]), slot(p), two(rstd[:, :]), ALU.mult).then_inc(freed[p], 1)

        for h in range(HEADS):
            dve.memset(AT[:, h, :], 0.0)
            distance(h, 0)
            distance(h, 1)
            decayed(h, 0)
            if h == 0:
                dve.wait_ge(sem["mask_in"], 16)
            for n, (kind, e) in enumerate((("v", 0), ("v", 1), ("r", 0), ("r", 1))):
                take_value(kind, h, e)
                dve.drain()
                keep(h, 2 * n)
                if n < 3:
                    distance(h, 2 * n + 2)
                decayed(h, 2 * n + 1)
                dve.drain()
                keep(h, 2 * n + 1)
                if n < 3:
                    distance(h, 2 * n + 3)
                decayed(h, 2 * n + 2)
            dve.drain()

        def finish(h):
            inverse_root(("head_norm", h), head_std, osum[:, :], DV)
            for e in range(2):
                dve.tensor_tensor(qk[:, 2 * h + e, :], o32[:, e, :], head_std,
                                  ALU.mult).then_inc(sem["o_scaled"], 1)

        dve.wait_ge(sem["dec_done"], HEADS)
        for h in range(HEADS):
            if h:
                dve.wait_ge(sem["chain_stored"], 16 * h)
            p = take(("U", h, 0))
            dve.tensor_copy(chain[:, 0, :], ps[:, p, 0:DV])
            dve.drain()
            for c in range(1, NCH):
                ins = dve.scalar_tensor_tensor(out=chain[:, c, :], in0=chain[:, c - 1, :],
                                               scalar=dec[:, h, c:c + 1], in1=ps[:, p, c * DV:(c + 1) * DV],
                                               op0=ALU.mult, op1=ALU.add)
                if c == NCH - 1:
                    ins.then_inc(freed[p], 1)
                dve.drain()
            dve.wait_ge(s0_in_s[h % 2], 16 * (h // 2 + 1))
            if h >= 2:
                dve.wait_ge(snew_stored[h % 2], 16)
            for s in range(SEQS):
                n = s % 4
                if n == 0:
                    p = take(("U", h, 1 + s // 4))
                ins = dve.scalar_tensor_tensor(out=snew[:, h % 2, s, :], in0=s0[:, h % 2, s, :],
                                               scalar=dec[:, h, 5 + s:6 + s], in1=ps[:, p, n * DV:(n + 1) * DV],
                                               op0=ALU.mult, op1=ALU.add)
                if n == 3:
                    ins.then_inc(freed[p], 1)
            p = take(("U", h, 3))
            dve.scalar_tensor_tensor(out=chain[:, 4, :], in0=chain[:, 3, :], scalar=dec[:, h, 4:5],
                                     in1=ps[:, p, 0:DV], op0=ALU.mult, op1=ALU.add).then_inc(freed[p], 1)
            if h:
                finish(h - 1)
            for e in range(2):
                p = take(("o", h, e))
                dve.wait_ge(sem["osq_done"], 2 * h + e + 1)
                if e == 0:
                    dve.drain()
                dve.scalar_tensor_tensor(out=o32[:, e, :], in0=ps[:, p, 0:TOK],
                                         scalar=par[:, C_GAIN + 2 * h + e:C_GAIN + 2 * h + e + 1],
                                         in1=sr[:, 2 * h + e, :], op0=ALU.mult,
                                         op1=ALU.mult).then_inc(freed[p], 1)
            dve.tensor_tensor(osum[:, :], osq[:, 0, :], osq[:, 1, :], ALU.add).then_inc(sem["osum_done"], 1)
        finish(HEADS - 1)
        dve.drain()
        dve.memset(zp[:, :, 0:2], 0.0)
        dve.wait_ge(sem["x_back"], 16)
        update_x(lambda m: ("w_out", m), 1)

        def convolve(src, out, w_col, bias):
            dve.tensor_scalar(out, src[:, 0:YN], w_col(0), w_col(3) if bias else None, ALU.mult,
                              ALU.add if bias else ALU.bypass)
            for j in (1, 2):
                dve.drain()
                last = dve.scalar_tensor_tensor(out=out, in0=src[:, j:j + YN], scalar=w_col(j), in1=out,
                                                op0=ALU.mult, op1=ALU.add)
            return last

        def gate_hidden(gate, f):
            up = y[:, 1, :]
            dve.tensor_tensor(hh[:, 0:PROMPT], gate[0][:, 0:PROMPT], up[:, 0:PROMPT], ALU.mult)
            dve.tensor_tensor(blocks(hh[:, PROMPT:TOK], SLEN), gate[1],
                              blocks(up[:, SB:PADDED], SW)[:, :, 0:SLEN], ALU.mult)
            dve.drain()
            dve.tensor_copy(gh[:, f, :], hh[:, :])
            dve.drain()
            dve.tensor_tensor(gl[:, f, :], hh[:, :], gh[:, f, :].bitcast(F32),
                              ALU.subtract).then_inc(sem["g_done"], 1)

        def take_padded(p, zi, factor, cut):
            if cut == HP:
                dve.tensor_tensor(zp[:, zi, 2:SB].rearrange("p (h t) -> p h t", h=2), slot(p, HP),
                                  factor[:, 0:PROMPT].rearrange("p (h t) -> p h t", h=2), ALU.mult)
            else:
                dve.tensor_tensor(zp[:, zi, 2:2 + cut], ps[:, p, 0:cut], factor[:, 0:cut], ALU.mult)
                dve.tensor_tensor(zp[:, zi, 2 + cut:SB], ps[:, p, BANK:BANK + PROMPT - cut],
                                  factor[:, cut:PROMPT], ALU.mult)
            a = BANK + PROMPT - cut
            dve.tensor_tensor(blocks(zp[:, zi, SB:PADDED], SW)[:, :, 2:SW], blocks(ps[:, p, a:a + SAMPLE], SLEN),
                              blocks(factor[:, PROMPT:TOK], SLEN), ALU.mult).then_inc(freed[p], 1)

        def z_unit(step, layer, z, j, i=0):
            zz = z + layer * ZT
            p = take(step, i)
            if not (isinstance(z, int) and zz < 4):
                dve.wait_ge(sem["zl_saved"], zz - 3)
            take_padded(p, j, rstd, HP)
            dve.drain()
            dve.wait_ge(sem["pads_in"], zz + 1)

            def col(c):
                return par[:, bass.ds(zz * 4 + (C_FFN + c), 1)]

            convolve(zp[:, j, :], y[:, j % 2, 0:YN], col, True).then_inc(sem["y_done"], 1)

        def group(layer, g, z0, i=0, f_count=None, late=True):
            for j in range(4):
                z_unit(("z", layer, g, j), layer, z0 + j, j, i)
                if j == 1 or j == 3 and not late:
                    gate_z(g, j, f_count)

        def gate_z(g, j, f_count):
            dve.drain()
            dve.wait_ge(sem["gate_silu"], f_count + (j + 1) // 2)
            gate_hidden((sg[:, :], blocks(sg[:, SB:PADDED], SW)[:, :, 0:SLEN]), 2 * (g % 2) + j // 2)

        def down(layer, g, i=0, late=None):
            for m in range(KT):
                if m == 2 and late:
                    late()
                p = take(("down", layer, g, m), i)
                dve.tensor_tensor(two(x[:, m, :]), slot(p), two(x[:, m, :]), ALU.add).then_inc(freed[p], 1)
            dve.drain()

        def gate_mix(E):
            dve.drain()
            gate_hidden((bg[:, E % 2, :], blocks(bg[:, E % 2, PROMPT:TOK], SLEN)), E % 4)

        def mixer():
            dve.wait_ge(sem["zl_saved"], ZT)
            for g in range(MIX_G + 1):
                if g < MIX_G:
                    for e in range(2):
                        E = 2 * g + e
                        dve.drain()
                        p = take(("mix", g, 3 * e))
                        dve.tensor_tensor(two(bg[:, e, :]), slot(p), two(rstd[:, :]),
                                          ALU.mult).then_inc(freed[p], 1)
                        p = take(("mix", g, 3 * e + 1))
                        dve.tensor_tensor(two(cg[:, :]), slot(p), two(rstd[:, :]), ALU.mult).then_inc(freed[p], 1)
                        dve.drain()
                        dve.tensor_tensor(cg[:, :], cg[:, :], rstd[:, :], ALU.mult)
                        dve.drain()
                        p = take(("mix", g, 3 * e + 2))
                        if E >= 2:
                            dve.wait_ge(sem["cl_saved"], E - 1)
                        take_padded(p, e, cg, HALF)
                        dve.drain()
                        dve.wait_ge(sem["cpads_in"], E + 1)
                        convolve(zp[:, e, :], y[:, 1, 0:YN],
                                 lambda c: par[:, C_SCW + 3 * E + c:C_SCW + 3 * E + c + 1],
                                 False).then_inc(sem["cy_done"], 1)
                        if e == 0 or g == 0:
                            gate_mix(E)
                if 1 <= g < MIX_G:
                    for m in range(KT):
                        if m == 2:
                            gate_mix(2 * g + 1)
                        p = take(("mix_out", g - 1, m))
                        dve.tensor_tensor(two(x[:, m, :]), slot(p), two(x[:, m, :]), ALU.add).then_inc(freed[p], 1)
                    dve.drain()
            update_x(lambda m: ("mix_out", MIX_G - 1, m), 3)

        for layer in range(2):
            n = 1 + 2 * layer
            if layer == 1:
                mixer()
                dve.wait_ge(sem["cl_saved"], KT)
            f0 = layer * FT
            invert_std(n)
            group(layer, 0, 0, f_count=f0, late=False)
            group(layer, 1, 4, f_count=f0 + 2)
            with dve.Fori(0, TRIPS) as i:
                for g in range(2):
                    count = 4 * i + (f0 + 2 + 2 * g)
                    down(layer, g, i, lambda: gate_z(1 + g, 3, count))
                    group(layer, 2 + g, 8 * i + (8 + 4 * g), i, count + 2)
            down(layer, 8, late=lambda: gate_z(9, 3, f0 + 18))
            group(layer, 10, 40, f_count=f0 + 20)
            down(layer, 9, late=lambda: gate_z(10, 3, f0 + 20))
            if layer == 0:
                update_x(lambda m: ("down", 0, 10, m), 2)
                invert_std(2)
        def add_last_square(c, m):
            dve.wait_ge(sem["sq_done"], KT * (4 + c) + m + 1)
            if m > 1:
                dve.drain()
            total = sq[:, 0, half(c)]
            return dve.tensor_tensor(total, total, sq[:, m, half(c)], ALU.add)

        for c in range(2):
            for m in range(KT):
                p = take(("last", c, m))
                dve.tensor_tensor(x[:, m, half(c)], bank(p, c), x[:, m, half(c)], ALU.add).then_inc(freed[p], 1)
                if m > 2:
                    add_last_square(c, m - 2)
            add_last_square(c, KT - 2)
            add_last_square(c, KT - 1).then_inc(sem["sum_done"], 1)
        for c in range(2):
            n_root = ROOT_ORDER.index(("last_norm", c))
            half_square(n_root, ("last_norm", c), cg[:, half(c)], D, c)
            refine(n_root, rstd[:, half(c)], cg[:, half(c)])
            dve.drain().then_inc(sem["final_std"], 1)
            for m in range(KT - POOL_OUT):
                dve.scalar_tensor_tensor(out=x[:, m, half(c)], in0=x[:, m, half(c)], scalar=norm_col(4, m),
                                         in1=rstd[:, half(c)], op0=ALU.mult,
                                         op1=ALU.mult).then_inc(sem["out_done"], 1)

    @block.scalar
    def _(act):
        def take(step, i=0):
            p, n = slots.at(step, i)
            act.wait_ge(filled[p], n + 1)
            return p

        def copied(step):
            p, n = slots.at(step)
            act.wait_ge(freed[p], n + 1)

        def split_high(n, m):
            act.activation(xh[:, m, :], x[:, m, :], ACT.Copy, scale=norm_col(n, m)).then_inc(sem["xs_hi"], 1)

        def square(n, m):
            act.activation((sq0 if n == 0 else sq)[:, m, :], x[:, m, :], ACT.Square).then_inc(sem["sq_done"], 1)

        def root(step, r, d, c=None):
            act.activation(tiny[:, :], ones[:, 0:1], ACT.Ln)
            p = take(step)
            out, src = (two(r), slot(p)) if c is None else (r, bank(p, c))
            act.activation(out, src, ACT.Ln, scale=1.0 / d,
                           bias=par[:, C_EPS:C_EPS + 1]).then_inc(sem["log_done"], 1)
            act.drain()
            act.activation(r, r, ACT.Exp, scale=-0.5).then_inc(sem["root_done"], 1)

        def norm_root(n):
            root(("norm", n), rstd[:, :], D)

        def head_root(h):
            root(("head_norm", h), head_std, DV)

        def split_out(h):
            for e in range(2):
                act.wait_ge(sem["o_scaled"], 2 * h + e + 1)
                act.activation(oh[:, 2 * h + e, :], qk[:, 2 * h + e, :],
                               ACT.Copy).then_inc(sem["oh_done"], 1)

        def norm_inputs(steps, n, u=None):
            for m in range(KT):
                copied(steps(m))
                split_high(n, m)
                square(n, m)
                if u is not None:
                    high(u + m)

        def high(u, i=0):
            if isinstance(u, int) and u >= N_UNITS:
                return
            j = u % RING
            act.wait_ge(landed[j], 16 * RING_TURNS * i + 16 * (u // RING + 1))
            if u >= RING:
                act.wait_ge(sem["units_used"], RING * RING_TURNS * i + (u - RING + 1))
            act.activation(wh[:, j, :, :], raw[:, j, :, :], ACT.Copy).then_inc(sem["hi_done"], 1)

        high(0)
        act.wait_ge(sem["consts"], 1)
        act.dma_start(wgd_raw[:, :, :], wgd_in).then_inc(sem["gla_in"], 16)
        act.dma_start(wgu[:, :], wgu_in).then_inc(sem["gla_in"], 16)
        act.wait_ge(sem["par_in"], 16)
        for m in range(KT):
            act.wait_ge(x_in_s[m], 16)
            split_high(0, m)
            if m == KT // 2:
                high(1)
            if m:
                square(0, m - 1)
        act.dma_start(reset[:, :], reset_in).then_inc(sem["gla_in"], 16)
        square(0, KT - 1)
        high(2)
        high(3)
        act.drain()
        act.wait_ge(sem["xs_lo"], KT)
        act.dma_start(mask_words[:, :], mask_in).then_inc(sem["mask_in"], 16)
        norm_root(0)
        high(4)
        high(5)

        for h in range(HEADS):
            copied(("gate_up", h))
            act.activation(soft[:, h, :], pre[:, h, :], ACT.Abs)
        act.drain()
        act.activation(soft[:, :, :], soft[:, :, :], ACT.Exp, scale=-1.0)
        act.drain()
        act.activation(soft[:, :, :], soft[:, :, :], ACT.Ln, bias=1.0).then_inc(sem["soft_done"], 1)
        for u in range(6, 2 * HEADS + RING):
            high(u)

        def decay(h, t):
            w = TOK if t >= 7 or LEVELS[t] < SLEN else TAIL
            e = dE[:, t % 2, 0:w]
            if t < 8:
                act.wait_ge(sem["d_done"], 8 * h + t + 1)
            if t < 7:
                act.activation(e, e, ACT.Abs)
                act.drain()
                act.activation(e, e, ACT.Exp, scale=-1.0 / TAU).then_inc(sem["e_done"], 1)
            elif t == 7:
                act.activation(e, e, ACT.Exp, scale=1.0 / TAU).then_inc(sem["e_done"], 1)
            else:
                act.wait_ge(sem["lev_done"], 9 * h + 7)
                act.activation(e, b[:, h, :], ACT.Exp, scale=1.0 / TAU).then_inc(sem["e_done"], 1)

        def v_to_tokens(h, e):
            p = take(("vT", h, e))
            c = (2 * h + e) * P
            act.copy(v_tok[:, :, c:c + P], blocks(ps[:, p, 0:6 * P], P)).then_inc(freed[p], 1)

        def k_to_tokens(h):
            p = take(("kT", h))
            act.copy(kd[:, 0:5, :], blocks(ps[:, p, 0:5 * P], P))
            for odd in range(2):
                last = act.activation(kd[:, 5 + odd, :], ps[:, p, 5 * P:6 * P], ACT.Copy,
                                      scale=par[:, C_EVEN + odd:C_EVEN + odd + 1])
            last.then_inc(freed[p], 1)

        def gate_r(h, e):
            copied(("r", h, e))
            act.activation(sr[:, 2 * h + e, :], stage[:, e, :], ACT.Silu).then_inc(sem["r_silu"], 1)

        for h in range(HEADS):
            u = 2 * HEADS + 4 * h + RING
            decay(h, 0)
            decay(h, 1)
            high(u)
            decay(h, 2)
            decay(h, 3)
            v_to_tokens(h, 0)
            high(u + 1)
            decay(h, 4)
            decay(h, 5)
            v_to_tokens(h, 1)
            if h == HEADS - 1:
                k_to_tokens(0)
            gate_r(h, 0)
            high(u + 2)
            decay(h, 6)
            decay(h, 7)
            gate_r(h, 1)
            if h + 1 < HEADS:
                high(u + 3)
            decay(h, 8)
            act.activation(dec[:, h, 0:4], blocks(b[:, h, 0:TAIL], CH)[:, :, CH - 1], ACT.Exp, scale=1.0 / TAU)
            act.activation(dec[:, h, 4:13], blocks(b[:, h, TAIL:TOK], SLEN)[:, :, SLEN - 1], ACT.Exp,
                           scale=1.0 / TAU).then_inc(sem["dec_done"], 1)

        def load_states(h):
            act.dma_start(s0[:, h % 2, :, :], s0_in[:, h, :, :]).then_inc(s0_in_s[h % 2], 16)

        take(("r", HEADS - 1, 1))
        load_states(0)
        load_states(1)
        act.wait_ge(sem["lev_done"], 9 * HEADS)
        copied(("A", HEADS - 1, 7))
        act.drain()
        act.dma_start(x[:, :, :], x_in).then_inc(sem["x_back"], 16)
        high(2 * HEADS + 16 + RING - 1)
        for h in range(HEADS):
            if h:
                head_root(h - 1)
            if h + 1 < HEADS:
                k_to_tokens(h + 1)
            copied(("U", h, 3))
            act.dma_start(sp_out[:, h, :], chain[:, 4, :]).then_inc(sem["chain_stored"], 16)
            act.dma_start(ss_out[:, h, :, :], snew[:, h % 2, :, :]).then_inc(snew_stored[h % 2], 16)
            for e in range(2):
                p = take(("o", h, e))
                if e == 0 and h:
                    act.wait_ge(sem["osum_done"], h)
                act.activation(osq[:, e, :], ps[:, p, 0:TOK], ACT.Square).then_inc(sem["osq_done"], 1)
            if h:
                split_out(h - 1)
            if h + 2 < HEADS:
                load_states(h + 2)
        act.dma_start(zc[:, :, :], zc_in).then_inc(sem["zc_in"], 16)
        head_root(HEADS - 1)
        split_out(HEADS - 1)
        act.wait_ge(sem["chain_stored"], 16 * HEADS)
        for i in range(2):
            act.wait_ge(snew_stored[i], 32)
        unit = 2 * HEADS + 16 + RING
        norm_inputs(lambda m: ("w_out", m), 1, unit)
        unit += KT

        def pads(z, j, layer):
            zz = z + layer * ZT
            act.copy(blocks(zp[:, j, SB:PADDED], SW)[:, :, 0:2],
                     zc[:, bass.ds(zz, 1), :].rearrange("p z (s w) -> p (z s) w", w=2)
                     ).then_inc(sem["pads_in"], 1)

        def z_unit(z, j, layer, more=True):
            zz = z + layer * ZT
            act.wait_ge(sem["y_done"], zz + 1)
            act.copy(zl[:, bass.ds(zz, 1), :].rearrange("p z (s w) -> p (z s) w", w=2),
                     blocks(zp[:, j, LAST:ZW], SW)[:, :, 0:2]).then_inc(sem["zl_saved"], 1)

        def gate(f_count):
            act.wait_ge(sem["g_done"], f_count[1])
            act.activation(sg[:, 0:YN], y[:, 0, 0:YN], ACT.Silu).then_inc(sem["gate_silu"], 1)

        act.wait_ge(sem["zc_in"], 16)
        g_before = 0
        for layer in range(2):
            if layer == 1:
                norm_inputs(lambda m: ("down", 0, GROUPS - 1, m), 2)
                high(unit)
                high(unit + 1)
                unit += 2
                for e in range(2):
                    act.copy(blocks(zp[:, e, SB:PADDED], SW)[:, :, 0:2],
                             par[:, C_CCACHE + 16 * e:C_CCACHE + 16 * e + 16].rearrange("p (s w) -> p s w", w=2)
                             ).then_inc(sem["cpads_in"], 1)
                high(unit)
                norm_root(2)
                high(unit + 1)
                act.dma_start(zl_out[:, 0:ZT, :], zl[:, 0:ZT, :]).then_inc(sem["tables_out"], 16)
                for g in range(MIX_G):
                    for e in range(2):
                        E = 2 * g + e
                        if E:
                            high(unit)
                            high(unit + 1)
                        act.wait_ge(sem["cy_done"], E + 1)
                        act.copy(cl[:, E, :].rearrange("p (s w) -> p s w", w=2),
                                 blocks(zp[:, E % 2, LAST:ZW], SW)[:, :, 0:2]).then_inc(sem["cl_saved"], 1)
                        if E + 2 < KT:
                            c = C_CCACHE + 16 * (E + 2)
                            act.copy(blocks(zp[:, E % 2, SB:PADDED], SW)[:, :, 0:2],
                                     par[:, c:c + 16].rearrange("p (s w) -> p s w", w=2)
                                     ).then_inc(sem["cpads_in"], 1)
                        high(unit + 2)
                        unit += 3
                    if g:
                        high(unit)
                        high(unit + 1)
                        unit += 2
                act.drain()
                act.dma_start(cl_out, cl[:, :, :]).then_inc(sem["tables_out"], 16)
                g_before += KT
                norm_inputs(lambda m: ("mix_out", MIX_G - 1, m), 3)
                high(unit)
                high(unit + 1)
                unit += 2
            for j in range(4):
                pads(j, j, layer)

            def z_group(z0, f, more, i=0):
                nonlocal unit
                for j in range(4):
                    z_unit(z0 + j, j, layer)
                    if j % 2 == 0:
                        gate((None, f + j // 2))
                    if more:
                        pads(z0 + j + 4, j, layer)
                    high(unit, i)
                    unit += 1

            def down_units(i=0):
                nonlocal unit
                high(unit, i)
                high(unit + 1, i)
                unit += 2

            high(unit)
            norm_root(1 + 2 * layer)
            high(unit + 1)
            for j in range(4):
                z_unit(j, j, layer)
                if j % 2 == 0:
                    gate((None, g_before + j // 2))
                pads(4 + j, j, layer)
                if j > 1:
                    high(unit + j)
            unit += 4
            z_group(4, g_before + 2, True)
            with act.Fori(0, TRIPS) as i:
                for g in range(2):
                    down_units(i)
                    z_group(8 * i + (8 + 4 * g), 2 * i + (g_before + 4 + 2 * g), True, i)
            unit += 12 * (TRIPS - 1)
            down_units()
            z_group(ZT - 4, g_before + FT - 2, False)
            down_units()
            act.drain()
            g_before += FT
        act.dma_start(zl_out[:, ZT:, :], zl[:, ZT:, :]).then_inc(sem["tables_out"], 16)

        def last_squares(c):
            for m in range(KT):
                copied(("last", c, m))
                act.activation(sq[:, m, half(c)], x[:, m, half(c)], ACT.Square).then_inc(sem["sq_done"], 1)

        def gain(c):
            act.drain()
            for m in range(KT - POOL_OUT, KT):
                act.activation(x[:, m, half(c)], x[:, m, half(c)], ACT.Copy,
                               scale=norm_col(4, m)).then_inc(sem["gained"], 1)

        def last_root(c):
            root(("last_norm", c), rstd[:, half(c)], D, c)

        act.activation(tiny[:, :], ones[:, 0:1], ACT.Ln)
        last_squares(0)
        gain(0)
        last_squares(1)
        last_root(0)
        last_root(1)
        gain(1)
        act.wait_ge(sem["tables_out"], 48)

    @block.sync
    def _(sp):
        by_dve = KT - POOL_OUT
        for c in range(2):
            for a, z in ((0, 2), (2, 4), (4, by_dve), (by_dve, by_dve + 2), (by_dve + 2, KT)):
                if z <= by_dve:
                    sp.wait_ge(sem["out_done"], by_dve * c + z)
                else:
                    sp.wait_ge(sem["pool_out"], POOL_OUT * c + z - by_dve)
                sp.dma_start(y_out[:, a:z, half(c)], x[:, a:z, half(c)]).then_inc(sem["written"], 16)
        sp.wait_ge(sem["written"], 16 * 10)

    block.__exit__(None, None, None)


def _units(w, cols):
    return [w[:, c:c + P].reshape(KT, P, P).transpose(1, 0, 2) for c in cols]


def _down_units(w, f):
    return [w[P * t:P * (t + 1), :].reshape(P, KT, P) for t in f]


def _weights(gla_w_in, gla_w_out, sc_w_in, sc_w_out, up, down):
    import numpy as np
    units = []
    for h in range(HEADS):
        units += _units(gla_w_in, [512 + P * h, P * h])
    for h in range(HEADS):
        units += _units(gla_w_in, [1024 + 256 * h, 1152 + 256 * h, 2048 + 256 * h, 2176 + 256 * h])
    units += _units(gla_w_out, [P * m for m in range(KT)])

    def ffn(layer):
        def z(g):
            return _units(up[layer], [P * f + FF * half for f in (2 * g, 2 * g + 1) for half in range(2)])

        def d(g):
            return _down_units(down[layer], (2 * g, 2 * g + 1))
        out = z(0) + z(1)
        for g in range(2, GROUPS):
            out += d(g - 2) + z(g)
        return out + d(GROUPS - 2) + d(GROUPS - 1)

    def mix_z(g):
        return _units(sc_w_in, [P * e + D * part for e in (2 * g, 2 * g + 1) for part in range(3)])

    units += ffn(0) + mix_z(0)
    for g in range(1, MIX_G):
        units += mix_z(g) + _down_units(sc_w_out, (2 * g - 2, 2 * g - 1))
    units += _down_units(sc_w_out, (2 * MIX_G - 2, 2 * MIX_G - 1)) + ffn(1)
    assert len(units) == N_UNITS
    return np.stack(units)


def _tiles(a):
    return a.T.reshape(-1, P, a.shape[0]).transpose(1, 0, 2)


def _masks():
    import numpy as np
    out = np.zeros((P, 8, TOK), np.uint8)
    for start, n in [(c * CH, CH) for c in range(NCH)] + [(TAIL, 16), (PROMPT, SAMPLE)]:
        s, t = np.arange(n)[:, None], np.arange(n)[None, :]
        out[:n, 0, start:start + n] = s == t
        for lv, m in enumerate(LEVELS):
            if m < SLEN or n == CH and start < TAIL:
                out[:n, lv + 1, start:start + n] = (s // (2 * m) == t // (2 * m)) & (s % (2 * m) < m) & (t % (2 * m) >= m)
    return out.reshape(P, -1).view(np.int32)


def kernel(**inputs):
    import numpy as np
    import concourse.bacc as bacc
    from concourse import mybir as mb
    from concourse.bass_utils import run_bass_kernel_spmd

    a = {k: np.ascontiguousarray(v) for k, v in inputs.items()}
    tokens = np.concatenate([a["meta"], a["x_prompt"][0], a["x_sample"].reshape(SAMPLE, D)])
    par = np.zeros((P, N_PAR), np.float32)
    norms = [a["norm_mix"][0], a["norm_ffn"][0], a["norm_mix"][1], a["norm_ffn"][1], a["norm_final"]]
    for n, g in enumerate(norms):
        par[:, C_NORM + 8 * n:C_NORM + 8 * n + 8] = g.reshape(KT, P).T
    par[:, C_BGATE:C_BGATE + 4] = a["gla_b_gate"][0].reshape(HEADS, P).T
    par[:, C_GAIN:C_GAIN + 8] = a["gla_head_gain"][0].reshape(KT, P).T
    par[:, C_SCW:C_SCW + 24] = a["sc_conv_w"][0].reshape(3, KT, P).transpose(2, 1, 0).reshape(P, 24)
    taps = np.concatenate([a["ffn_conv_w"], a["ffn_conv_b"][:, None, :]], axis=1)
    par[:, C_FFN:C_CCACHE] = taps.reshape(2, 4, 2, FT, P).transpose(4, 0, 3, 2, 1).reshape(P, -1)
    par[:, C_CCACHE:C_EVEN] = a["cache_conv"][0].reshape(SEQS, 2, KT, P).transpose(3, 2, 0, 1).reshape(P, -1)
    par[:, C_EVEN] = np.arange(P) // SLEN % 2 == 0
    par[:, C_ODD] = np.arange(P) // SLEN % 2
    par[:, C_EPS], par[:, C_HALF_EPS] = EPS, -0.5 * EPS
    wgd = a["gla_w_in"][0][:, 3072:3088].reshape(KT, P, 16).transpose(1, 0, 2)
    wgu = np.concatenate([a["gla_w_gate_up"][0]] * 2)
    reset = np.ones((P, TOK), np.float32)
    reset[:, 0:TAIL:CH] = 0
    reset[:, TAIL:TOK:SLEN] = 0
    zc = a["cache_ffn"].reshape(2, SEQS, 2, 2, FT, P).transpose(5, 0, 4, 3, 1, 2).reshape(P, 2 * ZT, 16)
    ins = {
        "x_t": _tiles(tokens), "w_units": _weights(a["gla_w_in"][0], a["gla_w_out"][0], a["sc_w_in"][0],
                                                   a["sc_w_out"][0], a["ffn_w_up"], a["ffn_w_down"]),
        "w_gate_down": wgd, "w_gate_up": wgu, "params": par, "scan_reset": reset, "level_masks": _masks(),
        "states": a["state_gla"][0].transpose(2, 1, 0, 3), "ffn_cache": zc,
    }
    outs = {"y_t": (P, KT, TOK), "state_prompt": (P, HEADS, DV), "state_sample": (P, HEADS, SEQS, DV),
            "ffn_last": (P, 2 * ZT, 18), "conv_last": (P, KT, 18)}
    nc = bacc.Bacc("TRN2", target_bir_lowering=False, num_devices=1)
    arrays, args = {}, []
    for name, v in ins.items():
        arrays[name] = np.ascontiguousarray(v)
        args.append(nc.dram_tensor(name, v.shape, mb.dt.from_np(v.dtype), kind="ExternalInput").ap())
    for name, shape in outs.items():
        args.append(nc.dram_tensor(name, shape, mb.dt.float32, kind="ExternalOutput").ap())
    build(nc, *args)
    got = run_bass_kernel_spmd(nc, [arrays], core_ids=[0]).results[0]

    y = got["y_t"].transpose(2, 1, 0).reshape(TOK, D)
    ffn = got["ffn_last"].reshape(P, 2, FT, 2, 1 + SEQS, 2).transpose(1, 4, 5, 3, 2, 0)
    ffn = ffn.reshape(2, 1 + SEQS, 2, 2 * FF)
    conv = got["conv_last"].reshape(P, KT, 1 + SEQS, 2).transpose(2, 3, 1, 0).reshape(1, 1 + SEQS, 2, D)
    c = np.ascontiguousarray
    return (c(y[16:PROMPT][None]), c(y[PROMPT:].reshape(SEQS, SLEN, D)),
            c(got["state_prompt"].transpose(1, 0, 2)[None, None]),
            c(got["state_sample"].transpose(2, 1, 0, 3)[None]),
            c(conv[:, :1]), c(conv[:, 1:]), c(ffn[:, :1]), c(ffn[:, 1:]))
```

```python
import concourse.bass as bass
from concourse import mybir

F32 = mybir.dt.float32
F32R = mybir.dt.float32r
U8 = mybir.dt.uint8
I32 = mybir.dt.int32
ALU = mybir.AluOpType
ACT = mybir.ActivationFunctionType

P = 128
D = 1024
KT = D // P
PROMPT = 16 + 512
SEQS, SLEN = 8, 16
SAMPLE = SEQS * SLEN
TOK = PROMPT + SAMPLE
HALF = TOK // 2
HEADS, DV = 4, 256
CH = 128
NCH = PROMPT // CH
TAIL = NCH * CH
FF = 2816
FT = FF // P
ZT = 2 * FT
PADDED = 2 + PROMPT + SEQS * (2 + SLEN)
SB = 2 + PROMPT
SW = 2 + SLEN
YN = PADDED - 2
LAST = PROMPT
ZW = LAST + (1 + SEQS) * SW
BANK = 512
RING = 4
TAU = 16.0
LEVELS = [1, 2, 4, 8, 16, 32, 64]
N_UNITS = 2 * HEADS + 16 + 8 + 2 * (ZT + FT) + 24 + 8
GROUPS = FT // 2
TRIPS = (GROUPS - 3) // 2
RING_TURNS = 3
STEP = 4
FIRST_ATT, FIRST_Z, FIRST_MIX = 8, (8, 12), 12
assert FIRST_Z[0] + STEP == FIRST_MIX == FIRST_Z[1]
META = 16
assert FIRST_Z[1] + STEP == META
POOL_SQ = [0, 2, 4]
POOL_OUT = 3
MIX_G = 4

C_NORM, C_BGATE, C_GAIN = 0, 40, 44
C_SCW = 52
C_FOURTH = 76
C_EPS, C_HALF_EPS = 80, 81
C_FFN = 82
C_CCACHE = C_FFN + 2 * ZT * 4
N_PAR = C_CCACHE + KT * 16
EPS = 1e-6
ROOT_ORDER = [("norm", 0)] + [("head_norm", h) for h in range(HEADS)] + [("norm", n) for n in range(1, 4)] + [("last_norm", c) for c in range(2)]


class SlotPlan:

    def __init__(self):
        self.used = [0] * RING
        self.next = 0
        self.steps = {}

    def straight(self, *names):
        for name in names:
            p = self.next % RING
            self.steps[name] = (p, self.used[p], 0)
            self.used[p] += 1
            self.next += 1

    def loop(self, names, trips):
        per = [0] * RING
        where = [(self.next + j) % RING for j in range(len(names))]
        for p in where:
            per[p] += 1
        seen = [0] * RING
        for name, p in zip(names, where):
            self.steps[name] = (p, self.used[p] + seen[p], per[p])
            seen[p] += 1
        for p in range(RING):
            self.used[p] += trips * per[p]
        self.next += len(names)

    def at(self, name, i=0):
        p, base, per = self.steps[name]
        return p, (base + per * i if per else base)


def plan_slots():
    s = SlotPlan()
    s.straight(("k", 0), ("q", 0), ("norm", 0), "gate_down")
    s.straight(("k", 1), *[("gate_up", h) for h in range(HEADS)])
    s.straight(("q", 1), *[(kind, h) for h in range(2, HEADS) for kind in "kq"])
    for h in range(HEADS):
        s.straight(("v", h, 0), ("A", h, 0), ("A", h, 1), ("v", h, 1), ("vT", h, 0), ("A", h, 2),
                   ("A", h, 3), ("r", h, 0), ("vT", h, 1))
        if h == HEADS - 1:
            s.straight(("kT", 0))
        s.straight(("A", h, 4), ("A", h, 5), ("r", h, 1), ("A", h, 6), ("A", h, 7))
    for h in range(HEADS):
        s.straight(("U", h, 0), ("U", h, 1), ("U", h, "tail"), ("U", h, 2))
        if h:
            s.straight(("head_norm", h - 1))
        if h + 1 < HEADS:
            s.straight(("kT", h + 1))
        s.straight(("o", h, 0), ("o", h, 1))
    s.straight(("w_out", 0), ("head_norm", HEADS - 1), *[("w_out", m) for m in range(1, KT)])
    for layer in range(2):
        if layer == 1:
            for g in range(MIX_G):
                for j in range(6):
                    s.straight(("mix", g, j))
                    if g == 0 and j == 1:
                        s.straight(("norm", 2))
                if g:
                    s.straight(*[("mix_out", g - 1, m) for m in range(KT)])
            s.straight(*[("mix_out", MIX_G - 1, m) for m in range(KT)])
        s.straight(("z", layer, 0, 0), ("z", layer, 0, 1), ("norm", 1 + 2 * layer),
                   ("z", layer, 0, 2), ("z", layer, 0, 3))
        s.straight(*[("z", layer, 1, j) for j in range(4)])
        body = []
        for g in range(2):
            body += [("down", layer, g, m) for m in range(KT)] + [("z", layer, 2 + g, j) for j in range(4)]
        s.loop(body, TRIPS)
        s.straight(*[("down", layer, 8, m) for m in range(KT)])
        s.straight(*[("z", layer, 10, j) for j in range(4)])
        s.straight(*[("down", layer, 9, m) for m in range(KT)])
        if layer == 0:
            s.straight(*[("down", layer, 10, m) for m in range(KT)])
    s.straight(*[("last", 0, m) for m in range(KT)], *[("last", 1, m) for m in range(KT - 1)], ("last_norm", 0),
               ("last", 1, KT - 1), ("last_norm", 1))
    return s


def build(nc, x_in, w_in, wgd_in, wgu_in, par_in, reset_in, mask_in, s0_in, zc_in,
          y_out, sp_out, ss_out, zl_out, cl_out):
    slots = plan_slots()

    base = (nc.sbuf_base + 31) // 32 * 32
    at = [base]

    def sb(name, shape, dt=F32, offset=None, size=None):
        if offset is not None:
            return nc.alloc_sbuf_tensor_at(name, shape, dt, offset=offset)
        n = 4
        for d in shape[1:]:
            n *= d
        t = nc.alloc_sbuf_tensor_at(name, shape, dt, offset=at[0])
        at[0] += (n + 31) // 32 * 32
        return t

    T4 = 4 * TOK
    x_at = at[0]
    x = sb("x", [P, KT, TOK])
    xh_at = at[0]
    xh = sb("xh", [P, KT, TOK], F32R)
    xl = sb("xl", [P, KT, TOK], F32R)
    raw = sb("raw", [P, RING, 8, P])
    wh = sb("wh", [P, RING, 8, P], F32R)
    wl = sb("wl", [P, RING, 8, P], F32R)
    par = sb("par", [P, N_PAR])
    rstd = sb("rstd", [P, TOK])
    ones = sb("ones", [P, P])
    tiny = sb("tiny", [P, 1])
    ident = sb("ident", [P, P])
    qk_at = at[0]
    qk = sb("qk", [P, 2 * HEADS, TOK])
    sr_at = at[0]
    sr = sb("sr", [P, KT, TOK])
    b_at = at[0]
    b = sb("b", [P, HEADS, TOK])
    vt_at = at[0]
    v_tok = sb("v_tok", [P, 6, D])
    AT_at = at[0]
    AT = sb("AT", [P, HEADS, TOK])
    osq = sb("osq", [P, 2, TOK])
    dec = sb("dec", [P, HEADS, 13])
    gla_end = at[0]
    reset = sb("reset", [P, TOK], offset=AT_at)
    gd = sb("gd", [P, TOK], offset=AT_at + T4)
    wgu = sb("wgu", [P, 512], offset=AT_at + 2 * T4)
    wgd_raw = sb("wgd_raw", [P, KT, 16], offset=AT_at + 2 * T4 + 2048)
    wgd = sb("wgd", [P, KT, 32], F32R, offset=AT_at + 2 * T4 + 2560)
    pre = sb("pre", [P, HEADS, TOK], offset=sr_at)
    soft = sb("soft", [P, HEADS, TOK], offset=sr_at + 4 * T4)
    sq0 = sb("sq0", [P, KT, TOK], offset=b_at)
    lev = sb("lev", [P, 2, TOK], offset=x_at)
    dE = sb("dE", [P, 2, TOK], offset=x_at + 2 * T4)
    stage = sb("stage", [P, 2, TOK], offset=x_at + 4 * T4)
    mask_words = sb("mask", [P, 8 * TOK // 4], I32, offset=x_at + 6 * T4)
    mask = mask_words[:, :].bitcast(U8).rearrange("p (l t) -> p l t", l=8)
    s0 = sb("s0", [P, 2, SEQS, DV], offset=xh_at)
    snew = sb("snew", [P, 2, SEQS, DV], offset=xh_at + 16384)
    o32 = sb("o32", [P, 2, TOK], offset=xh_at + 32768)
    osum = sb("osum", [P, TOK], offset=xh_at + 32768 + 2 * T4)
    kd = sb("kd", [P, 9, P], offset=b_at)
    chain = sb("chain", [P, 5, DV], offset=b_at + 9 * 4 * P)
    assert 9 * 4 * P + 5 * 4 * DV <= HEADS * T4
    head_std = AT[:, 0, :]
    oh = sb("oh", [P, KT, TOK], F32R, offset=sr_at)
    ol = sb("ol", [P, KT, TOK], F32R, offset=qk_at)
    at[0] = qk_at
    gh = sb("gh", [P, 4, TOK], F32R)
    gl = sb("gl", [P, 4, TOK], F32R)
    assert at[0] <= sr_at
    at[0] = sr_at
    y = sb("y", [P, 2, PADDED])
    sg = sb("sg", [P, PADDED])
    hh = sb("hh", [P, TOK])
    cg = sb("cg", [P, TOK])
    bg = sb("bg", [P, 2, TOK])
    assert at[0] <= b_at
    at[0] = b_at
    sq = sb("sq", [P, KT, TOK])
    zc = sb("zc", [P, 2 * ZT, 16])
    zl = sb("zl", [P, 2 * ZT, 18])
    cl = sb("cl", [P, KT, 18])
    zp = sb("zp", [P, 4, ZW])
    at[0] = max(at[0], gla_end)
    assert at[0] <= nc.sbuf_top

    ps = nc.alloc_psum_tensor("ps", [P, RING, 2 * BANK], F32)

    names = ["par_in", "more_par_in", "gla_in", "wgd_done", "hi_done", "lo_done", "units_used", "consts",
             "xs_hi", "xs_lo", "sq_done", "pool_sq_done", "sum_done", "log_done", "root_done", "soft_done", "mask_in", "d_done", "e_done",
             "lev_done", "r_silu", "dec_done", "chain_stored", "osq_done", "osum_done", "o_done", "o_scaled", "oh_done", "x_back",
             "zc_in", "pads_in", "y_done", "zl_saved", "gate_silu", "g_done", "cpads_in", "cy_done",
             "cl_saved", "out_done", "pool_out", "gained", "final_std", "written", "tables_out"]
    sem = {n: nc.alloc_semaphore(n) for n in names}
    filled = [nc.alloc_semaphore(f"filled{i}") for i in range(RING)]
    freed = [nc.alloc_semaphore(f"freed{i}") for i in range(RING)]
    landed = [nc.alloc_semaphore(f"landed{i}") for i in range(RING)]
    x_in_s = [nc.alloc_semaphore(f"x_in{i}") for i in range(KT)]
    snew_stored = [nc.alloc_semaphore(f"snew_stored{i}") for i in range(2)]
    s0_in_s = [nc.alloc_semaphore(f"s0_in{i}") for i in range(2)]

    def two(ap):
        return ap.rearrange("p (h t) -> p h t", h=2)

    def slot(p, n=HALF):
        return ps[:, p, :].rearrange("p (h t) -> p h t", h=2)[:, :, 0:n]

    def blocks(ap, n):
        return ap.rearrange("p (n t) -> p n t", t=n)

    def later(ap, m):
        return blocks(ap, 2 * m)[:, :, m:2 * m]

    def middle(first, end=TOK):
        return first + (end - first) // 2

    def banks(first, cut):
        return (0, first, cut), (BANK, cut, TOK)

    OUT_HALF = (TOK - META) // 2

    def half(c):
        return slice(META + c * OUT_HALF, META + (c + 1) * OUT_HALF)

    def bank(p, c):
        return ps[:, p, c * BANK:c * BANK + OUT_HALF]

    def from_token(first, ap, p):
        return two(ap[:, first:TOK]), slot(p, (TOK - first) // 2)

    def norm_col(n, m):
        return par[:, C_NORM + 8 * n + m:C_NORM + 8 * n + m + 1]

    block = nc.Block()
    block.__enter__()

    @block.sync
    def _(sp):
        sp.dma_start(raw[:, 0, :, :], w_in[0]).then_inc(landed[0], 16)
        sp.dma_start(par[:, 0:C_FFN], par_in[:, 0:C_FFN]).then_inc(sem["par_in"], 16)
        for k in range(KT):
            sp.dma_start(x[:, k, :], x_in[:, k, :]).then_inc(x_in_s[k], 16)
            if k == KT - 3:
                sp.dma_start(raw[:, 1, :, :], w_in[1]).then_inc(landed[1], 16)
        sp.dma_start(par[:, C_FFN:], par_in[:, C_FFN:]).then_inc(sem["more_par_in"], 16)
        for j in (2, 3):
            sp.dma_start(raw[:, j, :, :], w_in[j]).then_inc(landed[j], 16)
        with sp.Fori(0, N_UNITS // RING - 1) as i:
            for j in range(RING):
                sp.wait_ge(sem["lo_done"], RING * i + j + 1)
                sp.dma_start(raw[:, j, :, :], w_in[bass.ds(RING * i + (RING + j), 1)]
                             .rearrange("u p m n -> p (u m) n")).then_inc(landed[j], 16)

    @block.gpsimd
    def _(pool):
        pool.memset(ones[:, :], 1.0)
        pool.memset(ident[:, :], 0.0)
        pool.memset(gd[:, :], 0.0)
        pool.memset(wgu[:, :], 0.0)
        pool.drain()
        pool.affine_select(out=ident[:, :], in_=ident[:, :], compare_op=ALU.not_equal, fill=1.0, base=0,
                           pattern=[[-1, P]], channel_multiplier=1).then_inc(sem["consts"], 1)

        def low(j, done):
            pool.wait_ge(sem["hi_done"], done)
            pool.tensor_tensor(wl[:, j, :, :], raw[:, j, :, :], wh[:, j, :, :].bitcast(F32),
                               ALU.subtract).then_inc(sem["lo_done"], 1)

        for n, m in enumerate(POOL_SQ):
            pool.wait_ge(x_in_s[m], 16)
            pool.tensor_tensor(sq0[:, m, :], x[:, m, :], x[:, m, :], ALU.mult).then_inc(sem["pool_sq_done"], 1)
        pool.wait_ge(sem["lo_done"], 1)
        for j in range(1, RING):
            low(j, j + 1)
        before_out = (2 * HEADS + 16) // RING
        with pool.Fori(0, before_out) as i:
            for j in range(RING):
                low(j, RING * i + (RING + j + 1))
        for k in range(KT):
            pool.wait_ge(sem["oh_done"], k + 1)
            pool.tensor_tensor(ol[:, k, :], qk[:, k, :], oh[:, k, :].bitcast(F32),
                               ALU.subtract).then_inc(sem["o_done"], 1)
        with pool.Fori(0, N_UNITS // RING - 1 - before_out) as i:
            for j in range(RING):
                low(j, RING * i + (RING * (1 + before_out) + j + 1))
        for c in range(2):
            pool.wait_ge(sem["gained"], POOL_OUT * (c + 1))
            pool.wait_ge(sem["final_std"], c + 1)
            for m in range(KT - POOL_OUT, KT):
                pool.tensor_tensor(x[:, m, half(c)], x[:, m, half(c)], rstd[:, half(c)],
                                   ALU.mult).then_inc(sem["pool_out"], 1)

    @block.tensor
    def _(pe):
        unit = [0]

        def open_slot(step, i=0):
            p, n = slots.at(step, i)
            if not (isinstance(n, int) and n == 0):
                pe.wait_ge(freed[p], n)
            return p

        def copied(step):
            p, n = slots.at(step)
            pe.wait_ge(freed[p], n + 1)

        def weights(n_ready):
            pe.wait_ge(sem["lo_done"], n_ready)

        def project(step, hi, lo, n_ready, ring, first=0, cut=HALF, i=0, release=1, before=None):
            p = open_slot(step, i)
            weights(n_ready)
            for k in range(KT):
                if before:
                    before(k)
                for w, v in ((wh, hi), (wh, lo), (wl, hi)):
                    for c, a, z in banks(first, cut):
                        mm = pe.matmul(ps[:, p, c:c + z - a], w[:, ring, k, :], v[:, k, a:z],
                                       start=(k == 0 and w is wh and v is hi),
                                       stop=(k == KT - 1 and w is wl))
                        if k == 0 and w is wh and v is hi and c and release:
                            mm.then_inc(sem["units_used"], release)
            mm.then_inc(filled[p], 1)

        def project_down(step, first, f0, n_ready, rings, i=0, release=1, g_count=None):
            weights(n_ready)
            pe.wait_ge(sem["g_done"], g_count)
            for m in range(KT):
                p = open_slot(step(m), i)
                for f in range(2):
                    for w, v in ((wh, gh), (wh, gl), (wl, gh)):
                        for c, a, z in banks(first, middle(first)):
                            mm = pe.matmul(ps[:, p, c:c + z - a], w[:, rings[f], m, :], v[:, f0 + f, a:z],
                                           start=(f == 0 and w is wh and v is gh), stop=(f == 1 and w is wl))
                            if m == 0 and f == 0 and w is wh and v is gh and c:
                                mm.then_inc(sem["units_used"], release)
                mm.then_inc(filled[p], 1)

        def norm_sum(n):
            p = open_slot(("norm", n))
            pe.wait_ge(sem["sum_done"], n + 1)
            src = sq0 if n == 0 else sq
            for c, a in ((0, 0), (BANK, HALF)):
                mm = pe.matmul(ps[:, p, c:c + HALF], ones[:, :], src[:, 0, a:a + HALF], start=True, stop=True)
            mm.then_inc(filled[p], 1)

        n_unit = 0

        def x_ready(n):
            return lambda k: pe.wait_ge(sem["xs_lo"], KT * n + k + 1)

        def norm_amid(n):
            return lambda k: norm_sum(n) if k == KT // 2 else None

        pe.wait_ge(sem["consts"], 1)
        for h in range(HEADS):
            for j, kind in enumerate("kq"):
                project((kind, h), xh, xl, n_unit + 1, n_unit % RING, release=1 if n_unit else 0,
                        before=(x_ready(0), norm_amid(0))[j] if h == 0 else None)
                n_unit += 1
                if (kind, h) == ("k", 1):
                    copied("gate_down")
                    pe.wait_ge(sem["gla_in"], 48)
                    for g in range(HEADS):
                        p = open_slot(("gate_up", g))
                        for c, a in ((0, 0), (BANK, HALF)):
                            mm = pe.matmul(ps[:, p, c:c + HALF], wgu[:, g * P:(g + 1) * P], gd[:, a:a + HALF],
                                           start=True, stop=True)
                        mm.then_inc(filled[p], 1)
            if h == 0:
                p = open_slot("gate_down")
                pe.wait_ge(sem["wgd_done"], 1)
                for k in range(KT):
                    for v in (xh, xl):
                        for c, a in ((0, 0), (BANK, HALF)):
                            mm = pe.matmul(ps[0:32, p, c:c + HALF], wgd[:, k, :], v[:, k, a:a + HALF],
                                           start=(k == 0 and v is xh), stop=(k == KT - 1 and v is xl))
                mm.then_inc(filled[p], 1)

        def scores(h, lv):
            p = open_slot(("A", h, lv))
            if lv == 0:
                ks, qs = qk[:, 2 * h, :], qk[:, 2 * h + 1, :]
                copied(("k", h))
                copied(("q", h))
            else:
                ks = qs = lev[:, (lv - 1) % 2, :]
                pe.wait_ge(sem["lev_done"], 9 * h + lv)
            def queries(ap, a, z):
                return later(ap[:, a:z], LEVELS[lv - 1]) if lv else ap[:, a:z]

            def product(a, z):
                return pe.matmul(queries(ps[:, p, :], a, z), ks[:, a:a + P], queries(qs, a, z), start=True, stop=True)

            for c in range(NCH):
                mm = product(c * CH, (c + 1) * CH)
            if lv == 0 or LEVELS[lv - 1] < SLEN:
                product(TAIL, PROMPT)
                mm = product(PROMPT, TOK)
            mm.then_inc(filled[p], 1)

        starts = [c * CH for c in range(NCH)] + [TAIL, PROMPT]

        def to_tokens(step, src):
            p = open_slot(step)
            for t, a in enumerate(starts):
                mm = pe.transpose(ps[:, p, t * P:(t + 1) * P], src[:, a:a + P], ident[:, :])
            mm.then_inc(filled[p], 1)

        def value(kind, h, e):
            nonlocal n_unit
            project((kind, h, e), xh, xl, n_unit + 1, n_unit % RING)
            n_unit += 1

        def transpose_v(h, e):
            copied(("v", h, e))
            to_tokens(("vT", h, e), stage[:, e, :])

        def transpose_k(h):
            pe.wait_ge(sem["lev_done"], 9 * h + 8)
            to_tokens(("kT", h), qk[:, 2 * h, :])

        for h in range(HEADS):
            value("v", h, 0)
            scores(h, 0)
            scores(h, 1)
            value("v", h, 1)
            transpose_v(h, 0)
            scores(h, 2)
            scores(h, 3)
            value("r", h, 0)
            transpose_v(h, 1)
            if h == HEADS - 1:
                transpose_k(0)
            scores(h, 4)
            scores(h, 5)
            value("r", h, 1)
            scores(h, 6)
            scores(h, 7)

        def update(h, j, n, lhsT, rhs):
            p, _ = slots.at(("U", h, j))
            return pe.matmul(ps[:, p, n * DV:(n + 1) * DV], lhsT, rhs, start=True, stop=True,
                             skip_group_check=True), p

        def head_norm(h):
            p = open_slot(("head_norm", h))
            pe.wait_ge(sem["osum_done"], h + 1)
            for c, a in ((0, 0), (BANK, HALF)):
                mm = pe.matmul(ps[:, p, c:c + HALF], ones[:, :], osum[:, a:a + HALF], start=True, stop=True)
            mm.then_inc(filled[p], 1)

        for h in range(HEADS):
            vs = slice(h * DV, (h + 1) * DV)
            copied(("kT", h))
            for e in range(2):
                copied(("vT", h, e))
            open_slot(("U", h, 0))
            for c in range(NCH):
                mm, p = update(h, 0, c, kd[:, c, :], v_tok[:, c, vs])
                if h == c == 0:
                    mm.then_inc(sem["units_used"], 1)
            mm.then_inc(filled[p], 1)
            for j in (1, 2):
                if j == 2:
                    open_slot(("U", h, "tail"))
                    mm, p = update(h, "tail", 0, kd[0:16, 4, :], v_tok[0:16, 4, vs])
                    mm.then_inc(filled[p], 1)
                open_slot(("U", h, j))
                for n in range(4):
                    s = 4 * (j - 1) + n
                    rows = slice(64 * (s // 4), 64 * (s // 4) + 64)
                    mm, p = update(h, j, n, kd[rows, 5 + s % 4, :], v_tok[rows, 5, vs])
                mm.then_inc(filled[p], 1)
            if h:
                head_norm(h - 1)
            if h + 1 < HEADS:
                transpose_k(h + 1)
            copied(("U", h, 0))
            pe.wait_ge(s0_in_s[h % 2], 16 * (h // 2 + 1))
            pe.wait_ge(sem["lev_done"], 9 * h + 9)
            copied(("A", h, 7))
            q = qk[:, 2 * h + 1, :]
            for e in range(2):
                p = open_slot(("o", h, e))
                es = slice(h * DV + e * P, h * DV + (e + 1) * P)
                ee = slice(e * P, (e + 1) * P)

                def mm_o(a, z, lhsT, rhs, start, stop):
                    return pe.matmul(ps[:, p, a:z], lhsT, rhs, start=start, stop=stop, skip_group_check=True)

                for c in range(NCH):
                    a, z = c * CH, (c + 1) * CH
                    mm_o(a, z, v_tok[:, c, es], AT[:, h, a:z], True, c == 0)
                    if c:
                        mm_o(a, z, chain[:, c - 1, ee], q[:, a:z], False, True)
                mm_o(TAIL, PROMPT, v_tok[0:16, 4, es], AT[0:16, h, TAIL:PROMPT], True, False)
                mm_o(TAIL, PROMPT, chain[:, 3, ee], q[:, TAIL:PROMPT], False, True)
                mm_o(PROMPT, TOK, v_tok[:, 5, es], AT[:, h, PROMPT:TOK], True, False)
                for s in range(SEQS):
                    a = PROMPT + s * SLEN
                    mm = mm_o(a, a + SLEN, s0[:, h % 2, s, ee], q[:, a:a + SLEN], False, s == SEQS - 1)
                mm.then_inc(filled[p], 1)
        EARLY = 3
        for m in range(EARLY):
            p = open_slot(("w_out", m))
            weights(n_unit + m + 1)
            for k in range(KT - 2):
                if m == 0:
                    pe.wait_ge(sem["o_done"], k + 1)
                for w, v in ((wh, oh), (wh, ol), (wl, oh)):
                    for c, a, z in banks(FIRST_ATT, middle(FIRST_ATT)):
                        pe.matmul(ps[:, p, c:c + z - a], w[:, (n_unit + m) % RING, k, :], v[:, k, a:z],
                                  start=(k == 0 and w is wh and v is oh), stop=False)
            if m == 0:
                head_norm(HEADS - 1)
        for m in range(EARLY):
            p, _ = slots.at(("w_out", m))
            for k in (KT - 2, KT - 1):
                pe.wait_ge(sem["o_done"], k + 1)
                for w, v in ((wh, oh), (wh, ol), (wl, oh)):
                    for c, a, z in banks(FIRST_ATT, middle(FIRST_ATT)):
                        mm = pe.matmul(ps[:, p, c:c + z - a], w[:, (n_unit + m) % RING, k, :], v[:, k, a:z],
                                       start=False, stop=(k == KT - 1 and w is wl))
                        if m and k == KT - 2 and c and w is wh and v is oh:
                            mm.then_inc(sem["units_used"], 1)
            mm.then_inc(filled[p], 1)
        n_unit += EARLY
        for m in range(EARLY, KT):
            project(("w_out", m), oh, ol, n_unit + 1, n_unit % RING, FIRST_ATT, middle(FIRST_ATT))
            n_unit += 1

        g_before = 0
        for layer in range(2):
            if layer == 1:
                for g in range(MIX_G):
                    for j in range(6):
                        project(("mix", g, j), xh, xl, n_unit + 1, n_unit % RING, FIRST_MIX, middle(FIRST_MIX),
                                release=2 if j == 0 and (g != 1) else 1,
                                before=(x_ready(2), norm_amid(2))[j] if g == 0 and j < 2 else None)
                        n_unit += 1
                    if g:
                        project_down(lambda m, g=g: ("mix_out", g - 1, m), FIRST_MIX, 2 * ((g - 1) % 2), n_unit + 2,
                                     [n_unit % RING, (n_unit + 1) % RING], g_count=g_before + 2 * g)
                        n_unit += 2
                project_down(lambda m: ("mix_out", MIX_G - 1, m), FIRST_MIX, 2 * ((MIX_G - 1) % 2), n_unit + 2,
                             [n_unit % RING, (n_unit + 1) % RING], release=2, g_count=g_before + 2 * MIX_G)
                n_unit += 2
                g_before += 2 * MIX_G
            def z_units(g, i=0, release=1, norm=None):
                nonlocal n_unit
                for j in range(4):
                    u = n_unit + j
                    project(("z", layer, g, j), xh, xl, 12 * i + (u + 1), u % RING, FIRST_Z[layer],
                            middle(FIRST_Z[layer], PROMPT), i=i,
                            release=release if j == 0 else 1,
                            before=(x_ready(norm), norm_amid(norm))[j] if norm is not None and j < 2 else None)
                n_unit += 4

            def down_units(g, count, i=0, release=1):
                nonlocal n_unit
                u = n_unit
                project_down(lambda m: ("down", layer, g, m), FIRST_Z[layer] + STEP, 2 * (g % 2), 12 * i + (u + 2),
                             [u % RING, (u + 1) % RING], i=i, release=release, g_count=count)
                n_unit += 2

            z_units(0, release=2 if layer else 1, norm=1 + 2 * layer)
            z_units(1)
            with nc.Fori(0, TRIPS, engines=[mybir.EngineType.PE], hint_back_edge=True) as i:
                for g in range(2):
                    down_units(g, 4 * i + (g_before + 2 * g + 2), i=i)
                    z_units(2 + g, i=i, release=2)
            n_unit += 12 * (TRIPS - 1)
            down_units(8, g_before + 18)
            z_units(10, release=2)
            down_units(9, g_before + 20)
            if layer == 0:
                down_units(10, g_before + 22, release=2)
            g_before += FT

        def last_norm(c):
            p = open_slot(("last_norm", c))
            pe.wait_ge(sem["sum_done"], 5 + c)
            pe.matmul(bank(p, c), ones[:, :], sq[:, 0, half(c)], start=True, stop=True).then_inc(filled[p], 1)

        weights(N_UNITS)
        pe.wait_ge(sem["g_done"], g_before)
        for c in range(2):
            for m in range(KT):
                p = open_slot(("last", c, m))
                for f in range(2):
                    for w, v in ((wh, gh), (wh, gl), (wl, gh)):
                        mm = pe.matmul(bank(p, c), w[:, (n_unit + f) % RING, m, :], v[:, f, half(c)],
                                       start=(f == 0 and w is wh and v is gh), stop=(f == 1 and w is wl))
                mm.then_inc(filled[p], 1)
                if c and m == KT - 2:
                    last_norm(0)
        last_norm(1)
        n_unit += 2
        assert n_unit == N_UNITS

    @block.vector
    def _(dve):
        def take(step, i=0):
            p, n = slots.at(step, i)
            dve.wait_ge(filled[p], n + 1)
            return p

        def split_low(n, m):
            dve.wait_ge(sem["xs_hi"], KT * n + m + 1)
            dve.scalar_tensor_tensor(out=xl[:, m, :], in0=x[:, m, :], scalar=norm_col(n, m),
                                     in1=xh[:, m, :].bitcast(F32), op0=ALU.mult,
                                     op1=ALU.subtract).then_inc(sem["xs_lo"], 1)

        def add_square(n, m):
            if m == 0:
                return
            if n:
                dve.wait_ge(sem["sq_done"], KT * n - len(POOL_SQ) + m + 1)
            else:
                dve.wait_ge(sem["pool_sq_done"], sum(t <= m for t in POOL_SQ))
                dve.wait_ge(sem["sq_done"], sum(t <= m and t not in POOL_SQ for t in range(KT)))
            if m > 1:
                dve.drain()
            total, src = (sq0 if n == 0 else sq)[:, 0, :], (sq0 if n == 0 else sq)[:, m, :]
            ins = dve.tensor_tensor(total, total, src, ALU.add)
            if m == KT - 1:
                ins.then_inc(sem["sum_done"], 1)

        def half_square(n_root, step, v, d, c=None):
            p = take(step)
            dve.wait_ge(sem["log_done"], n_root + 1)
            out, src = (two(v), slot(p)) if c is None else (v, bank(p, c))
            dve.tensor_scalar(out, src, -0.5 / d, par[:, C_HALF_EPS:C_HALF_EPS + 1], ALU.mult,
                              ALU.add).then_inc(freed[p], 1)

        def refine(n_root, r, v):
            dve.wait_ge(sem["root_done"], n_root + 1)
            dve.drain()
            dve.tensor_tensor(v, v, r, ALU.mult)
            dve.drain()
            dve.tensor_tensor(v, v, r, ALU.mult)
            dve.drain()
            dve.scalar_tensor_tensor(out=r, in0=v, scalar=1.5, in1=r, op0=ALU.add, op1=ALU.mult)
            dve.drain()

        def inverse_root(step, r, v, d):
            half_square(ROOT_ORDER.index(step), step, v, d)
            refine(ROOT_ORDER.index(step), r, v)

        def invert_std(n):
            inverse_root(("norm", n), rstd[:, :], osq[:, 1, :] if n == 0 else cg[:, :], D)

        def add_to_x(p, m, first):
            tile, product = from_token(first, x[:, m, :], p)
            dve.tensor_tensor(tile, product, tile, ALU.add).then_inc(freed[p], 1)

        def update_x(steps, first, n):
            for m in range(KT):
                p = take(steps(m))
                add_to_x(p, m, first)
                if m:
                    split_low(n, m - 1)
                    if n == 1:
                        add_square(n, m - 1)
            split_low(n, KT - 1)
            for m in [KT - 1] if n == 1 else range(KT):
                add_square(n, m)

        dve.wait_ge(sem["hi_done"], 1)
        dve.tensor_tensor(wl[:, 0, :, :], raw[:, 0, :, :], wh[:, 0, :, :].bitcast(F32),
                          ALU.subtract).then_inc(sem["lo_done"], 1)

        dve.wait_ge(sem["par_in"], 16)
        for m in range(KT):
            split_low(0, m)
            if 2 <= m < KT - 2:
                add_square(0, m - 2)
        for m in range(KT - 4, KT):
            add_square(0, m)
        dve.wait_ge(sem["gla_in"], 48)
        dve.tensor_copy(wgd[:, :, 0:16], wgd_raw[:, :, :])
        dve.drain()
        dve.tensor_tensor(wgd[:, :, 16:32], wgd_raw[:, :, :], wgd[:, :, 0:16].bitcast(F32),
                          ALU.subtract).then_inc(sem["wgd_done"], 1)
        invert_std(0)

        def take_k(h):
            p = take(("k", h))
            dve.tensor_tensor(two(qk[:, 2 * h, :]), slot(p), two(rstd[:, :]), ALU.mult).then_inc(freed[p], 1)

        def take_q(h):
            p = take(("q", h))
            dve.scalar_tensor_tensor(out=two(qk[:, 2 * h + 1, :]), in0=slot(p), scalar=float(P) ** -0.5,
                                     in1=two(rstd[:, :]), op0=ALU.mult, op1=ALU.mult).then_inc(freed[p], 1)

        take_k(0)
        take_q(0)
        p = take("gate_down")
        dve.tensor_tensor(two(gd[0:32, :]), slot(p)[0:32], two(rstd[0:32, :]), ALU.mult).then_inc(freed[p], 1)
        take_k(1)
        for h in range(HEADS):
            p = take(("gate_up", h))
            dve.tensor_scalar(two(pre[:, h, :]), slot(p), par[:, C_BGATE + h:C_BGATE + h + 1], None,
                              ALU.add).then_inc(freed[p], 1)
        take_q(1)
        dve.wait_ge(sem["soft_done"], 1)
        dve.scalar_tensor_tensor(out=pre[:, :, :], in0=pre[:, :, :], scalar=0.0, in1=soft[:, :, :],
                                 op0=ALU.min, op1=ALU.subtract)
        dve.drain()
        for h in range(HEADS):
            dve.tensor_tensor_scan(b[:, h, :], reset[:, :], pre[:, h, :], 0.0, ALU.mult, ALU.add)
        dve.drain()
        for h in (2, 3):
            take_k(h)
            take_q(h)

        def width(t):
            return TOK if LEVELS[t] < SLEN else TAIL

        def distance(h, t):
            if t < 7:
                m, w = LEVELS[t], width(t)
                bb = blocks(b[:, h, 0:w], 2 * m)
                ref = bb[:, :, m - 1:m].to_broadcast([P, w // (2 * m), 2 * m])
                dve.tensor_tensor(blocks(dE[:, t % 2, 0:w], 2 * m), bb, ref,
                                  ALU.subtract).then_inc(sem["d_done"], 1)
                return
            for a, z, m in ((0, TAIL, CH), (TAIL, TOK, SLEN)):
                bb = blocks(b[:, h, a:z], m)
                ref = bb[:, :, m - 1:m].to_broadcast([P, (z - a) // m, m])
                last = dve.tensor_tensor(blocks(dE[:, t % 2, a:z], m), ref, bb, ALU.subtract)
            last.then_inc(sem["d_done"], 1)

        def decayed(h, t):
            dve.wait_ge(sem["e_done"], 9 * h + t + 1)
            k, q = qk[:, 2 * h, :], qk[:, 2 * h + 1, :]
            if t < 7:
                m, w = LEVELS[t], width(t)
                for src, part in ((k, slice(0, m)), (q, slice(m, 2 * m))):
                    last = dve.tensor_tensor(blocks(lev[:, t % 2, 0:w], 2 * m)[:, :, part],
                                             blocks(dE[:, t % 2, 0:w], 2 * m)[:, :, part],
                                             blocks(src[:, 0:w], 2 * m)[:, :, part], ALU.mult)
            else:
                src = k if t == 7 else q
                last = dve.tensor_tensor(src, src, dE[:, t % 2, :], ALU.mult)
            last.then_inc(sem["lev_done"], 1)

        def keep(h, lv):
            p = take(("A", h, lv))
            if lv == 0:
                out, m, src = AT[:, h, :], mask[:, 0, :], ps[:, p, 0:TOK]
            else:
                out, m, src = (later(a[:, 0:width(lv - 1)], LEVELS[lv - 1])
                               for a in (AT[:, h, :], mask[:, lv, :], ps[:, p, :]))
            dve.copy_predicated(out, m, src).then_inc(freed[p], 1)

        def take_value(kind, h, e):
            if kind == "v" and h:
                dve.wait_ge(sem["r_silu"], 2 * (h - 1) + e + 1)
            if kind == "r":
                take(("vT", h, e))
            p = take((kind, h, e))
            dve.tensor_tensor(two(stage[:, e, :]), slot(p), two(rstd[:, :]), ALU.mult).then_inc(freed[p], 1)

        for h in range(HEADS):
            if h == 0:
                dve.memset(AT[:, h, :], 0.0)
            distance(h, 0)
            distance(h, 1)
            decayed(h, 0)
            if h == 0:
                dve.wait_ge(sem["mask_in"], 16)
            for n, (kind, e) in enumerate((("v", 0), ("v", 1), ("r", 0), ("r", 1))):
                take_value(kind, h, e)
                dve.drain()
                keep(h, 2 * n)
                if n < 3:
                    distance(h, 2 * n + 2)
                decayed(h, 2 * n + 1)
                dve.drain()
                keep(h, 2 * n + 1)
                if n == 2 and h + 1 < HEADS:
                    dve.memset(AT[:, h + 1, :], 0.0)
                if n < 3:
                    distance(h, 2 * n + 3)
                decayed(h, 2 * n + 2)
            dve.drain()

        def finish(h):
            inverse_root(("head_norm", h), head_std, osum[:, :], DV)
            for e in range(2):
                dve.tensor_tensor(qk[:, 2 * h + e, :], o32[:, e, :], head_std,
                                  ALU.mult).then_inc(sem["o_scaled"], 1)

        dve.wait_ge(sem["dec_done"], HEADS)
        for h in range(HEADS):
            if h:
                dve.wait_ge(sem["chain_stored"], 16 * h)
            p = take(("U", h, 0))
            dve.tensor_copy(chain[:, 0, :], ps[:, p, 0:DV])
            dve.drain()
            for c in range(1, NCH):
                ins = dve.scalar_tensor_tensor(out=chain[:, c, :], in0=chain[:, c - 1, :],
                                               scalar=dec[:, h, c:c + 1], in1=ps[:, p, c * DV:(c + 1) * DV],
                                               op0=ALU.mult, op1=ALU.add)
                if c == NCH - 1:
                    ins.then_inc(freed[p], 1)
                dve.drain()
            dve.wait_ge(s0_in_s[h % 2], 16 * (h // 2 + 1))
            if h >= 2:
                dve.wait_ge(snew_stored[h % 2], 16)
            for s in range(SEQS):
                n = s % 4
                if n == 0:
                    p = take(("U", h, 1 + s // 4))
                ins = dve.scalar_tensor_tensor(out=snew[:, h % 2, s, :], in0=s0[:, h % 2, s, :],
                                               scalar=dec[:, h, 5 + s:6 + s], in1=ps[:, p, n * DV:(n + 1) * DV],
                                               op0=ALU.mult, op1=ALU.add)
                if n == 3:
                    ins.then_inc(freed[p], 1)
                if s == 3:
                    p = take(("U", h, "tail"))
                    dve.scalar_tensor_tensor(out=chain[:, 4, :], in0=chain[:, 3, :], scalar=dec[:, h, 4:5],
                                             in1=ps[:, p, 0:DV], op0=ALU.mult, op1=ALU.add).then_inc(freed[p], 1)
            if h:
                finish(h - 1)
            for e in range(2):
                p = take(("o", h, e))
                dve.wait_ge(sem["osq_done"], 2 * h + e + 1)
                if e == 0:
                    dve.drain()
                dve.scalar_tensor_tensor(out=o32[:, e, :], in0=ps[:, p, 0:TOK],
                                         scalar=par[:, C_GAIN + 2 * h + e:C_GAIN + 2 * h + e + 1],
                                         in1=sr[:, 2 * h + e, :], op0=ALU.mult,
                                         op1=ALU.mult).then_inc(freed[p], 1)
            dve.tensor_tensor(osum[:, :], osq[:, 0, :], osq[:, 1, :], ALU.add).then_inc(sem["osum_done"], 1)
        finish(HEADS - 1)
        dve.wait_ge(sem["x_back"], 16)
        dve.wait_ge(sem["more_par_in"], 16)
        update_x(lambda m: ("w_out", m), FIRST_ATT, 1)

        def convolve(src, out, first, w_col, bias):
            out = out[:, first:YN]
            dve.tensor_scalar(out, src[:, first:YN], w_col(0), w_col(3) if bias else None, ALU.mult,
                              ALU.add if bias else ALU.bypass)
            for j in (1, 2):
                dve.drain()
                last = dve.scalar_tensor_tensor(out=out, in0=src[:, first + j:YN + j], scalar=w_col(j), in1=out,
                                                op0=ALU.mult, op1=ALU.add)
            return last

        def gate_hidden(gate, f, first):
            up = y[:, 1, :]
            dve.tensor_tensor(hh[:, first:PROMPT], gate[0][:, first:PROMPT], up[:, first:PROMPT], ALU.mult)
            dve.tensor_tensor(blocks(hh[:, PROMPT:TOK], SLEN), gate[1],
                              blocks(up[:, SB:PADDED], SW)[:, :, 0:SLEN], ALU.mult)
            dve.drain()
            dve.tensor_copy(gh[:, f, first:TOK], hh[:, first:TOK])
            dve.drain()
            dve.tensor_tensor(gl[:, f, first:TOK], hh[:, first:TOK], gh[:, f, first:TOK].bitcast(F32),
                              ALU.subtract).then_inc(sem["g_done"], 1)

        def take_padded(p, zi, factor, first, cut):
            if cut == middle(first, PROMPT):
                dve.tensor_tensor(two(zp[:, zi, 2 + first:SB]), slot(p, cut - first), two(factor[:, first:PROMPT]),
                                  ALU.mult)
            else:
                dve.tensor_tensor(zp[:, zi, 2 + first:2 + cut], ps[:, p, 0:cut - first], factor[:, first:cut],
                                  ALU.mult)
                dve.tensor_tensor(zp[:, zi, 2 + cut:SB], ps[:, p, BANK:BANK + PROMPT - cut],
                                  factor[:, cut:PROMPT], ALU.mult)
            a = BANK + PROMPT - cut
            dve.tensor_tensor(blocks(zp[:, zi, SB:PADDED], SW)[:, :, 2:SW], blocks(ps[:, p, a:a + SAMPLE], SLEN),
                              blocks(factor[:, PROMPT:TOK], SLEN), ALU.mult).then_inc(freed[p], 1)

        def z_unit(step, layer, z, j, i=0):
            zz = z + layer * ZT
            p = take(step, i)
            if not (isinstance(z, int) and zz < 4):
                dve.wait_ge(sem["zl_saved"], zz - 3)
            take_padded(p, j, rstd, FIRST_Z[layer], middle(FIRST_Z[layer], PROMPT))
            dve.drain()
            dve.wait_ge(sem["pads_in"], zz + 1)

            def col(c):
                return par[:, bass.ds(zz * 4 + (C_FFN + c), 1)]

            convolve(zp[:, j, :], y[:, j % 2, :], FIRST_Z[layer] + STEP, col, True).then_inc(sem["y_done"], 1)

        def group(layer, g, z0, i=0, f_count=None, late=True):
            for j in range(4):
                z_unit(("z", layer, g, j), layer, z0 + j, j, i)
                if j == 1 or j == 3 and not late:
                    gate_z(layer, g, j, f_count)

        def gate_z(layer, g, j, f_count):
            dve.drain()
            dve.wait_ge(sem["gate_silu"], f_count + (j + 1) // 2)
            gate_hidden((sg[:, :], blocks(sg[:, SB:PADDED], SW)[:, :, 0:SLEN]), 2 * (g % 2) + j // 2,
                        FIRST_Z[layer] + STEP)

        def down(layer, g, i=0, late=None):
            for m in range(KT):
                if m == 2 and late:
                    late()
                add_to_x(take(("down", layer, g, m), i), m, FIRST_Z[layer] + STEP)
            dve.drain()

        def gate_mix(E):
            dve.drain()
            gate_hidden((bg[:, E % 2, :], blocks(bg[:, E % 2, PROMPT:TOK], SLEN)), E % 4, FIRST_MIX)

        def mixer():
            dve.wait_ge(sem["zl_saved"], ZT)
            for g in range(MIX_G + 1):
                if g < MIX_G:
                    for e in range(2):
                        E = 2 * g + e
                        dve.drain()
                        p = take(("mix", g, 3 * e))
                        out, product = from_token(FIRST_MIX, bg[:, e, :], p)
                        dve.tensor_tensor(out, product, two(rstd[:, FIRST_MIX:]), ALU.mult).then_inc(freed[p], 1)
                        p = take(("mix", g, 3 * e + 1))
                        out, product = from_token(FIRST_MIX, cg, p)
                        dve.tensor_tensor(out, product, two(rstd[:, FIRST_MIX:]), ALU.mult).then_inc(freed[p], 1)
                        dve.drain()
                        dve.tensor_tensor(cg[:, FIRST_MIX:], cg[:, FIRST_MIX:], rstd[:, FIRST_MIX:], ALU.mult)
                        dve.drain()
                        p = take(("mix", g, 3 * e + 2))
                        if E >= 2:
                            dve.wait_ge(sem["cl_saved"], E - 1)
                        take_padded(p, e, cg, FIRST_MIX, middle(FIRST_MIX))
                        dve.drain()
                        dve.wait_ge(sem["cpads_in"], E + 1)
                        convolve(zp[:, e, :], y[:, 1, :], FIRST_MIX,
                                 lambda c: par[:, C_SCW + 3 * E + c:C_SCW + 3 * E + c + 1],
                                 False).then_inc(sem["cy_done"], 1)
                        if e == 0 or g == 0:
                            gate_mix(E)
                if 1 <= g < MIX_G:
                    for m in range(KT):
                        if m == 2:
                            gate_mix(2 * g + 1)
                        add_to_x(take(("mix_out", g - 1, m)), m, FIRST_MIX)
                    dve.drain()
            update_x(lambda m: ("mix_out", MIX_G - 1, m), FIRST_MIX, 3)

        for layer in range(2):
            n = 1 + 2 * layer
            if layer == 1:
                mixer()
                dve.wait_ge(sem["cl_saved"], KT)
            f0 = layer * FT
            invert_std(n)
            group(layer, 0, 0, f_count=f0, late=False)
            group(layer, 1, 4, f_count=f0 + 2)
            with dve.Fori(0, TRIPS) as i:
                for g in range(2):
                    count = 4 * i + (f0 + 2 + 2 * g)
                    down(layer, g, i, lambda: gate_z(layer, 1 + g, 3, count))
                    group(layer, 2 + g, 8 * i + (8 + 4 * g), i, count + 2)
            down(layer, 8, late=lambda: gate_z(layer, 9, 3, f0 + 18))
            group(layer, 10, 40, f_count=f0 + 20)
            down(layer, 9, late=lambda: gate_z(layer, 10, 3, f0 + 20))
            if layer == 0:
                update_x(lambda m: ("down", 0, 10, m), FIRST_Z[0] + STEP, 2)
                invert_std(2)
        def add_last_square(c, m):
            dve.wait_ge(sem["sq_done"], KT * (4 + c) - len(POOL_SQ) + m + 1)
            if m > 1:
                dve.drain()
            total = sq[:, 0, half(c)]
            return dve.tensor_tensor(total, total, sq[:, m, half(c)], ALU.add)

        for c in range(2):
            for m in range(KT):
                p = take(("last", c, m))
                dve.tensor_tensor(x[:, m, half(c)], bank(p, c), x[:, m, half(c)], ALU.add).then_inc(freed[p], 1)
                if m > 2:
                    add_last_square(c, m - 2)
            add_last_square(c, KT - 2)
            add_last_square(c, KT - 1).then_inc(sem["sum_done"], 1)
        for c in range(2):
            n_root = ROOT_ORDER.index(("last_norm", c))
            half_square(n_root, ("last_norm", c), cg[:, half(c)], D, c)
            refine(n_root, rstd[:, half(c)], cg[:, half(c)])
            dve.drain().then_inc(sem["final_std"], 1)
            for m in range(KT - POOL_OUT):
                dve.scalar_tensor_tensor(out=x[:, m, half(c)], in0=x[:, m, half(c)], scalar=norm_col(4, m),
                                         in1=rstd[:, half(c)], op0=ALU.mult,
                                         op1=ALU.mult).then_inc(sem["out_done"], 1)

    @block.scalar
    def _(act):
        def take(step, i=0):
            p, n = slots.at(step, i)
            act.wait_ge(filled[p], n + 1)
            return p

        def copied(step):
            p, n = slots.at(step)
            act.wait_ge(freed[p], n + 1)

        def split_high(n, m):
            act.activation(xh[:, m, :], x[:, m, :], ACT.Copy, scale=norm_col(n, m)).then_inc(sem["xs_hi"], 1)

        def square(n, m):
            act.activation((sq0 if n == 0 else sq)[:, m, :], x[:, m, :], ACT.Square).then_inc(sem["sq_done"], 1)

        def root(step, r, d, c=None):
            act.activation(tiny[:, :], ones[:, 0:1], ACT.Ln)
            p = take(step)
            out, src = (two(r), slot(p)) if c is None else (r, bank(p, c))
            act.activation(out, src, ACT.Ln, scale=1.0 / d,
                           bias=par[:, C_EPS:C_EPS + 1]).then_inc(sem["log_done"], 1)
            act.drain()
            act.activation(r, r, ACT.Exp, scale=-0.5).then_inc(sem["root_done"], 1)

        def norm_root(n):
            root(("norm", n), rstd[:, :], D)

        def head_root(h):
            root(("head_norm", h), head_std, DV)

        def split_out(h):
            for e in range(2):
                act.wait_ge(sem["o_scaled"], 2 * h + e + 1)
                act.activation(oh[:, 2 * h + e, :], qk[:, 2 * h + e, :],
                               ACT.Copy).then_inc(sem["oh_done"], 1)

        def norm_inputs(steps, n, u=None):
            for m in range(KT):
                copied(steps(m))
                split_high(n, m)
                square(n, m)
                if u is not None:
                    high(u + m)

        def high(u, i=0):
            if isinstance(u, int) and u >= N_UNITS:
                return
            j = u % RING
            act.wait_ge(landed[j], 16 * RING_TURNS * i + 16 * (u // RING + 1))
            if u >= RING:
                act.wait_ge(sem["units_used"], RING * RING_TURNS * i + (u - RING + 1))
            act.activation(wh[:, j, :, :], raw[:, j, :, :], ACT.Copy).then_inc(sem["hi_done"], 1)

        high(0)
        act.wait_ge(sem["consts"], 1)
        act.dma_start(wgd_raw[:, :, :], wgd_in).then_inc(sem["gla_in"], 16)
        act.dma_start(wgu[0:32, :], wgu_in).then_inc(sem["gla_in"], 16)
        act.wait_ge(sem["par_in"], 16)
        for m in range(KT):
            act.wait_ge(x_in_s[m], 16)
            split_high(0, m)
            if m == KT - 2:
                high(1)
            if m and m - 1 not in POOL_SQ:
                square(0, m - 1)
        act.dma_start(reset[:, :], reset_in).then_inc(sem["gla_in"], 16)
        square(0, KT - 1)
        high(2)
        high(3)
        act.drain()
        act.wait_ge(sem["xs_lo"], KT)
        act.dma_start(mask_words[:, :], mask_in).then_inc(sem["mask_in"], 16)
        norm_root(0)
        high(4)
        high(5)

        for h in range(HEADS):
            copied(("gate_up", h))
            act.activation(soft[:, h, :], pre[:, h, :], ACT.Abs)
        act.drain()
        act.activation(soft[:, :, :], soft[:, :, :], ACT.Exp, scale=-1.0)
        act.drain()
        act.activation(soft[:, :, :], soft[:, :, :], ACT.Ln, bias=1.0).then_inc(sem["soft_done"], 1)
        for u in range(6, 2 * HEADS + RING):
            high(u)

        def decay(h, t):
            w = TOK if t >= 7 or LEVELS[t] < SLEN else TAIL
            e = dE[:, t % 2, 0:w]
            if t < 8:
                act.wait_ge(sem["d_done"], 8 * h + t + 1)
            if t < 7:
                act.activation(e, e, ACT.Abs)
                act.drain()
                act.activation(e, e, ACT.Exp, scale=-1.0 / TAU).then_inc(sem["e_done"], 1)
            elif t == 7:
                act.activation(e, e, ACT.Exp, scale=1.0 / TAU).then_inc(sem["e_done"], 1)
            else:
                act.wait_ge(sem["lev_done"], 9 * h + 7)
                act.activation(e, b[:, h, :], ACT.Exp, scale=1.0 / TAU).then_inc(sem["e_done"], 1)

        def v_to_tokens(h, e):
            p = take(("vT", h, e))
            c = (2 * h + e) * P
            act.copy(v_tok[:, :, c:c + P], blocks(ps[:, p, 0:6 * P], P)).then_inc(freed[p], 1)

        def k_to_tokens(h):
            p = take(("kT", h))
            act.copy(kd[:, 0:5, :], blocks(ps[:, p, 0:5 * P], P))
            for j in range(4):
                last = act.activation(kd[:, 5 + j, :], ps[:, p, 5 * P:6 * P], ACT.Copy,
                                      scale=par[:, C_FOURTH + j:C_FOURTH + j + 1])
            last.then_inc(freed[p], 1)

        def gate_r(h, e):
            copied(("r", h, e))
            act.activation(sr[:, 2 * h + e, :], stage[:, e, :], ACT.Silu).then_inc(sem["r_silu"], 1)

        for h in range(HEADS):
            u = 2 * HEADS + 4 * h + RING
            decay(h, 0)
            decay(h, 1)
            high(u)
            decay(h, 2)
            decay(h, 3)
            v_to_tokens(h, 0)
            high(u + 1)
            decay(h, 4)
            decay(h, 5)
            v_to_tokens(h, 1)
            if h == HEADS - 1:
                k_to_tokens(0)
            gate_r(h, 0)
            high(u + 2)
            decay(h, 6)
            decay(h, 7)
            gate_r(h, 1)
            if h + 1 < HEADS:
                high(u + 3)
            decay(h, 8)
            act.activation(dec[:, h, 0:4], blocks(b[:, h, 0:TAIL], CH)[:, :, CH - 1], ACT.Exp, scale=1.0 / TAU)
            act.activation(dec[:, h, 4:13], blocks(b[:, h, TAIL:TOK], SLEN)[:, :, SLEN - 1], ACT.Exp,
                           scale=1.0 / TAU).then_inc(sem["dec_done"], 1)

        def load_states(h):
            act.dma_start(s0[:, h % 2, :, :], s0_in[:, h, :, :]).then_inc(s0_in_s[h % 2], 16)

        take(("r", HEADS - 1, 1))
        load_states(0)
        load_states(1)
        act.wait_ge(sem["lev_done"], 9 * HEADS)
        copied(("A", HEADS - 1, 7))
        act.drain()
        act.dma_start(x[:, :, :], x_in).then_inc(sem["x_back"], 16)
        high(2 * HEADS + 16 + RING - 1)
        for h in range(HEADS):
            if h:
                head_root(h - 1)
            if h + 1 < HEADS:
                k_to_tokens(h + 1)
            copied(("U", h, 2))
            act.dma_start(sp_out[:, h, :], chain[:, 4, :]).then_inc(sem["chain_stored"], 16)
            act.dma_start(ss_out[:, h, :, :], snew[:, h % 2, :, :]).then_inc(snew_stored[h % 2], 16)
            for e in range(2):
                p = take(("o", h, e))
                if e == 0 and h:
                    act.wait_ge(sem["osum_done"], h)
                act.activation(osq[:, e, :], ps[:, p, 0:TOK], ACT.Square).then_inc(sem["osq_done"], 1)
            if h:
                split_out(h - 1)
            if h + 2 < HEADS:
                load_states(h + 2)
        act.dma_start(zc[:, :, :], zc_in).then_inc(sem["zc_in"], 16)
        head_root(HEADS - 1)
        split_out(HEADS - 1)
        act.wait_ge(sem["chain_stored"], 16 * HEADS)
        for i in range(2):
            act.wait_ge(snew_stored[i], 32)
        unit = 2 * HEADS + 16 + RING
        norm_inputs(lambda m: ("w_out", m), 1, unit)
        unit += KT

        def pads(z, j, layer):
            zz = z + layer * ZT
            act.copy(blocks(zp[:, j, SB:PADDED], SW)[:, :, 0:2],
                     zc[:, bass.ds(zz, 1), :].rearrange("p z (s w) -> p (z s) w", w=2)
                     ).then_inc(sem["pads_in"], 1)

        def z_unit(z, j, layer):
            zz = z + layer * ZT
            act.wait_ge(sem["y_done"], zz + 1)
            act.copy(zl[:, bass.ds(zz, 1), :].rearrange("p z (s w) -> p (z s) w", w=2),
                     blocks(zp[:, j, LAST:ZW], SW)[:, :, 0:2]).then_inc(sem["zl_saved"], 1)

        def gate(layer, count):
            act.wait_ge(sem["g_done"], count)
            row = slice(FIRST_Z[layer] + STEP, YN)
            act.activation(sg[:, row], y[:, 0, row], ACT.Silu).then_inc(sem["gate_silu"], 1)

        act.wait_ge(sem["zc_in"], 16)
        act.wait_ge(sem["more_par_in"], 16)
        g_before = 0
        for layer in range(2):
            if layer == 1:
                norm_inputs(lambda m: ("down", 0, GROUPS - 1, m), 2)
                high(unit)
                high(unit + 1)
                unit += 2
                for e in range(2):
                    act.copy(blocks(zp[:, e, SB:PADDED], SW)[:, :, 0:2],
                             par[:, C_CCACHE + 16 * e:C_CCACHE + 16 * e + 16].rearrange("p (s w) -> p s w", w=2)
                             ).then_inc(sem["cpads_in"], 1)
                high(unit)
                norm_root(2)
                high(unit + 1)
                act.dma_start(zl_out[:, 0:ZT, :], zl[:, 0:ZT, :]).then_inc(sem["tables_out"], 16)
                for g in range(MIX_G):
                    for e in range(2):
                        E = 2 * g + e
                        if E:
                            high(unit)
                            high(unit + 1)
                        act.wait_ge(sem["cy_done"], E + 1)
                        act.copy(cl[:, E, :].rearrange("p (s w) -> p s w", w=2),
                                 blocks(zp[:, E % 2, LAST:ZW], SW)[:, :, 0:2]).then_inc(sem["cl_saved"], 1)
                        if E + 2 < KT:
                            c = C_CCACHE + 16 * (E + 2)
                            act.copy(blocks(zp[:, E % 2, SB:PADDED], SW)[:, :, 0:2],
                                     par[:, c:c + 16].rearrange("p (s w) -> p s w", w=2)
                                     ).then_inc(sem["cpads_in"], 1)
                        high(unit + 2)
                        unit += 3
                    if g:
                        high(unit)
                        high(unit + 1)
                        unit += 2
                act.drain()
                act.dma_start(cl_out, cl[:, :, :]).then_inc(sem["tables_out"], 16)
                g_before += KT
                norm_inputs(lambda m: ("mix_out", MIX_G - 1, m), 3)
                high(unit)
                high(unit + 1)
                unit += 2
            for j in range(4):
                pads(j, j, layer)

            def z_group(z0, f, more, i=0):
                nonlocal unit
                for j in range(4):
                    z_unit(z0 + j, j, layer)
                    if j % 2 == 0:
                        gate(layer, f + j // 2)
                    if more:
                        pads(z0 + j + 4, j, layer)
                    high(unit, i)
                    unit += 1

            def down_units(i=0):
                nonlocal unit
                high(unit, i)
                high(unit + 1, i)
                unit += 2

            high(unit)
            norm_root(1 + 2 * layer)
            high(unit + 1)
            for j in range(4):
                z_unit(j, j, layer)
                if j % 2 == 0:
                    gate(layer, g_before + j // 2)
                pads(4 + j, j, layer)
                if j > 1:
                    high(unit + j)
            unit += 4
            z_group(4, g_before + 2, True)
            with act.Fori(0, TRIPS) as i:
                for g in range(2):
                    down_units(i)
                    z_group(8 * i + (8 + 4 * g), 2 * i + (g_before + 4 + 2 * g), True, i)
            unit += 12 * (TRIPS - 1)
            down_units()
            z_group(ZT - 4, g_before + FT - 2, False)
            down_units()
            act.drain()
            g_before += FT
        act.dma_start(zl_out[:, ZT:, :], zl[:, ZT:, :]).then_inc(sem["tables_out"], 16)

        def last_squares(c):
            for m in range(KT):
                copied(("last", c, m))
                act.activation(sq[:, m, half(c)], x[:, m, half(c)], ACT.Square).then_inc(sem["sq_done"], 1)

        def gain(c):
            act.drain()
            for m in range(KT - POOL_OUT, KT):
                act.activation(x[:, m, half(c)], x[:, m, half(c)], ACT.Copy,
                               scale=norm_col(4, m)).then_inc(sem["gained"], 1)

        def last_root(c):
            root(("last_norm", c), rstd[:, half(c)], D, c)

        act.activation(tiny[:, :], ones[:, 0:1], ACT.Ln)
        last_squares(0)
        gain(0)
        last_squares(1)
        last_root(0)
        last_root(1)
        gain(1)
        act.wait_ge(sem["tables_out"], 48)

    @block.sync
    def _(sp):
        by_dve = KT - POOL_OUT
        for c in range(2):
            for a, z in ((0, 2), (2, 4), (4, by_dve), (by_dve, by_dve + 2), (by_dve + 2, KT)):
                if z <= by_dve:
                    sp.wait_ge(sem["out_done"], by_dve * c + z)
                else:
                    sp.wait_ge(sem["pool_out"], POOL_OUT * c + z - by_dve)
                sp.dma_start(y_out[:, a:z, c * OUT_HALF:(c + 1) * OUT_HALF], x[:, a:z, half(c)]).then_inc(sem["written"], 16)
        sp.wait_ge(sem["written"], 16 * 10)

    block.__exit__(None, None, None)


def _units(w, cols):
    return [w[:, c:c + P].reshape(KT, P, P).transpose(1, 0, 2) for c in cols]


def _down_units(w, f):
    return [w[P * t:P * (t + 1), :].reshape(P, KT, P) for t in f]


def _weights(gla_w_in, gla_w_out, sc_w_in, sc_w_out, up, down):
    import numpy as np
    units = []
    for h in range(HEADS):
        units += _units(gla_w_in, [512 + P * h, P * h])
    for h in range(HEADS):
        units += _units(gla_w_in, [1024 + 256 * h, 1152 + 256 * h, 2048 + 256 * h, 2176 + 256 * h])
    units += _units(gla_w_out, [P * m for m in range(KT)])

    def ffn(layer):
        def z(g):
            return _units(up[layer], [P * f + FF * half for f in (2 * g, 2 * g + 1) for half in range(2)])

        def d(g):
            return _down_units(down[layer], (2 * g, 2 * g + 1))
        out = z(0) + z(1)
        for g in range(2, GROUPS):
            out += d(g - 2) + z(g)
        return out + d(GROUPS - 2) + d(GROUPS - 1)

    def mix_z(g):
        return _units(sc_w_in, [P * e + D * part for e in (2 * g, 2 * g + 1) for part in range(3)])

    units += ffn(0) + mix_z(0)
    for g in range(1, MIX_G):
        units += mix_z(g) + _down_units(sc_w_out, (2 * g - 2, 2 * g - 1))
    units += _down_units(sc_w_out, (2 * MIX_G - 2, 2 * MIX_G - 1)) + ffn(1)
    assert len(units) == N_UNITS
    return np.stack(units)


def _tiles(a):
    return a.T.reshape(-1, P, a.shape[0]).transpose(1, 0, 2)


def _masks():
    import numpy as np
    out = np.zeros((P, 8, TOK), np.uint8)
    for start, n in [(c * CH, CH) for c in range(NCH)] + [(TAIL, 16), (PROMPT, SAMPLE)]:
        s, t = np.arange(n)[:, None], np.arange(n)[None, :]
        out[:n, 0, start:start + n] = s == t
        for lv, m in enumerate(LEVELS):
            if m < SLEN or n == CH and start < TAIL:
                out[:n, lv + 1, start:start + n] = (s // (2 * m) == t // (2 * m)) & (s % (2 * m) < m) & (t % (2 * m) >= m)
    return out.reshape(P, -1).view(np.int32)


def kernel(**inputs):
    import numpy as np
    import concourse.bacc as bacc
    from concourse import mybir as mb
    from concourse.bass_utils import run_bass_kernel_spmd

    a = {k: np.ascontiguousarray(v) for k, v in inputs.items()}
    tokens = np.concatenate([a["meta"], a["x_prompt"][0], a["x_sample"].reshape(SAMPLE, D)])
    par = np.zeros((P, N_PAR), np.float32)
    norms = [a["norm_mix"][0], a["norm_ffn"][0], a["norm_mix"][1], a["norm_ffn"][1], a["norm_final"]]
    for n, g in enumerate(norms):
        par[:, C_NORM + 8 * n:C_NORM + 8 * n + 8] = g.reshape(KT, P).T
    par[:, C_BGATE:C_BGATE + 4] = a["gla_b_gate"][0].reshape(HEADS, P).T
    par[:, C_GAIN:C_GAIN + 8] = a["gla_head_gain"][0].reshape(KT, P).T
    par[:, C_SCW:C_SCW + 24] = a["sc_conv_w"][0].reshape(3, KT, P).transpose(2, 1, 0).reshape(P, 24)
    taps = np.concatenate([a["ffn_conv_w"], a["ffn_conv_b"][:, None, :]], axis=1)
    par[:, C_FFN:C_CCACHE] = taps.reshape(2, 4, 2, FT, P).transpose(4, 0, 3, 2, 1).reshape(P, -1)
    par[:, C_CCACHE:N_PAR] = a["cache_conv"][0].reshape(SEQS, 2, KT, P).transpose(3, 2, 0, 1).reshape(P, -1)
    for j in range(4):
        par[:, C_FOURTH + j] = np.arange(P) // SLEN % 4 == j
    par[:, C_EPS], par[:, C_HALF_EPS] = EPS, -0.5 * EPS
    wgd = a["gla_w_in"][0][:, 3072:3088].reshape(KT, P, 16).transpose(1, 0, 2)
    wgu = np.concatenate([a["gla_w_gate_up"][0]] * 2)
    reset = np.ones((P, TOK), np.float32)
    reset[:, 0:TAIL:CH] = 0
    reset[:, TAIL:TOK:SLEN] = 0
    zc = a["cache_ffn"].reshape(2, SEQS, 2, 2, FT, P).transpose(5, 0, 4, 3, 1, 2).reshape(P, 2 * ZT, 16)
    ins = {
        "x_t": _tiles(tokens), "w_units": _weights(a["gla_w_in"][0], a["gla_w_out"][0], a["sc_w_in"][0],
                                                   a["sc_w_out"][0], a["ffn_w_up"], a["ffn_w_down"]),
        "w_gate_down": wgd, "w_gate_up": wgu, "params": par, "scan_reset": reset, "level_masks": _masks(),
        "states": a["state_gla"][0].transpose(2, 1, 0, 3), "ffn_cache": zc,
    }
    outs = {"y_t": (P, KT, TOK - META), "state_prompt": (P, HEADS, DV), "state_sample": (P, HEADS, SEQS, DV),
            "ffn_last": (P, 2 * ZT, 18), "conv_last": (P, KT, 18)}
    nc = bacc.Bacc("TRN2", target_bir_lowering=False, num_devices=1)
    arrays, args = {}, []
    for name, v in ins.items():
        arrays[name] = np.ascontiguousarray(v)
        args.append(nc.dram_tensor(name, v.shape, mb.dt.from_np(v.dtype), kind="ExternalInput").ap())
    for name, shape in outs.items():
        args.append(nc.dram_tensor(name, shape, mb.dt.float32, kind="ExternalOutput").ap())
    build(nc, *args)
    got = run_bass_kernel_spmd(nc, [arrays], core_ids=[0]).results[0]

    y = got["y_t"].transpose(2, 1, 0).reshape(TOK - META, D)
    ffn = got["ffn_last"].reshape(P, 2, FT, 2, 1 + SEQS, 2).transpose(1, 4, 5, 3, 2, 0)
    ffn = ffn.reshape(2, 1 + SEQS, 2, 2 * FF)
    conv = got["conv_last"].reshape(P, KT, 1 + SEQS, 2).transpose(2, 3, 1, 0).reshape(1, 1 + SEQS, 2, D)
    c = np.ascontiguousarray
    return (c(y[:PROMPT - META][None]), c(y[PROMPT - META:].reshape(SEQS, SLEN, D)),
            c(got["state_prompt"].transpose(1, 0, 2)[None, None]),
            c(got["state_sample"].transpose(2, 1, 0, 3)[None]),
            c(conv[:, :1]), c(conv[:, 1:]), c(ffn[:, :1]), c(ffn[:, 1:]))
```
